# Optimizing a Trainium2 kernel written in Bass

```python
import jax, jax.numpy as jnp
from jax import lax
import numpy as np

D_MODEL = 1024
BATCH = 1
SEQ = 2048
DEPTH = 1

GRID_W = 64
NA_W = D_MODEL // 2
NA_HEAD_DIM = 64
NA_HEADS = NA_W // NA_HEAD_DIM
NA_KH = 8
NA_KW = 16
ML_W = D_MODEL // 2
ML_HEADS = 4
ML_HEAD_DIM = ML_W // ML_HEADS
MIX_W = NA_W + ML_W
ML_CHUNK = 64
CONV_W = 5
EPS = 1e-6
IN_SPLITS = (NA_W,) * 4 + (ML_W,) * 5 + (ML_HEADS,) * 4
IN_W = 4 * NA_W + 5 * ML_W + 4 * ML_HEADS


def rmsnorm(x, w):
    x32 = x.astype(jnp.float32)
    return x32 * lax.rsqrt(jnp.mean(x32 * x32, axis=-1, keepdims=True) + EPS) * w

def centred_short_conv(u, w, b):
    T = u.shape[1]
    pad = CONV_W // 2
    up = jnp.pad(u, ((0, 0), (pad, pad), (0, 0)))
    out = up[:, 0:T] * w[0]
    for j in range(1, CONV_W):
        out = out + up[:, j:j + T] * w[j]
    return out + b

def neighbourhood_attention(q, k, v, rpb):
    B, T, _ = q.shape
    rows = T // GRID_W
    kh = min(NA_KH, rows)

    def to_grid(t):
        return t.reshape(B, rows, GRID_W, NA_HEADS, NA_HEAD_DIM).transpose(0, 3, 1, 2, 4)

    qg = to_grid(q) * (NA_HEAD_DIM ** -0.5)
    kgrid, vgrid = to_grid(k), to_grid(v)
    r = jnp.arange(rows)
    row_idx = jnp.clip(r - kh // 2, 0, rows - kh)[:, None] + jnp.arange(kh)[None, :]
    kg = kgrid[:, :, row_idx]
    vg = vgrid[:, :, row_idx]
    col = jnp.arange(GRID_W)
    col_start = jnp.clip(col - NA_KW // 2, 0, GRID_W - NA_KW)
    col_mask = (col[None, :] >= col_start[:, None]) & (col[None, :] < col_start[:, None] + NA_KW)
    dy = row_idx - r[:, None] + NA_KH - 1
    dx = jnp.clip(col[None, :] - col[:, None], -(NA_KW - 1), NA_KW - 1) + NA_KW - 1
    bias = rpb[:, dy[:, None, :, None], dx[None, :, None, :]]
    s = jnp.einsum('bhrcd,bhrjkd->bhrcjk', qg, kg).astype(jnp.float32) + bias[None]
    s = jnp.where(col_mask[:, None, :], s, -jnp.inf)
    p = jax.nn.softmax(s.reshape(B, NA_HEADS, rows, GRID_W, kh * GRID_W), axis=-1).reshape(s.shape)
    o = jnp.einsum('bhrcjk,bhrjkd->bhrcd', p, vg)
    return o.transpose(0, 2, 3, 1, 4).reshape(B, T, NA_W)

def mlstm_chunkwise(q, k, v, i_pre, f_pre):
    B, H, T, d = q.shape
    L = ML_CHUNK
    nc = T // L
    q = q.reshape(B, H, nc, L, d)
    k = (k * (d ** -0.5)).reshape(B, H, nc, L, d)
    v = v.reshape(B, H, nc, L, d)
    i_pre = i_pre.reshape(B, H, nc, L)
    b = jnp.cumsum(jax.nn.log_sigmoid(f_pre).reshape(B, H, nc, L), axis=-1)
    b_last = b[..., -1]
    a = b_last[..., None] - b + i_pre

    def step(carry, inp):
        C, n, m = carry
        k_c, v_c, a_c, bl_c = inp
        m_new = jnp.maximum(bl_c + m, jnp.max(a_c, axis=-1))
        decay = jnp.exp(bl_c + m - m_new)
        w = jnp.exp(a_c - m_new[..., None])
        C_new = decay[..., None, None] * C + jnp.einsum('bhs,bhse,bhsd->bhed', w, v_c, k_c)
        n_new = decay[..., None] * n + jnp.einsum('bhs,bhsd->bhd', w, k_c)
        return (C_new, n_new, m_new), (C, n, m)

    init = (jnp.zeros((B, H, d, d), q.dtype), jnp.zeros((B, H, d), q.dtype), jnp.zeros((B, H), q.dtype))
    xs = (jnp.moveaxis(k, 2, 0), jnp.moveaxis(v, 2, 0), jnp.moveaxis(a, 2, 0), jnp.moveaxis(b_last, 2, 0))
    _, (C_prev, n_prev, m_prev) = lax.scan(step, init, xs)
    C_prev = jnp.moveaxis(C_prev, 0, 2)
    n_prev = jnp.moveaxis(n_prev, 0, 2)
    m_prev = jnp.moveaxis(m_prev, 0, 2)

    lower = jnp.tril(jnp.ones((L, L), dtype=bool))
    Dlog = jnp.where(lower, b[..., :, None] - b[..., None, :] + i_pre[..., None, :], -jnp.inf)
    m_inter = b + m_prev[..., None]
    m_t = jnp.maximum(m_inter, jnp.max(Dlog, axis=-1))
    S = jnp.einsum('bhntd,bhnsd->bhnts', q, k) * jnp.exp(Dlog - m_t[..., None])
    inter = jnp.exp(m_inter - m_t)
    num = jnp.einsum('bhnts,bhnse->bhnte', S, v) + inter[..., None] * jnp.einsum('bhned,bhntd->bhnte', C_prev, q)
    den = jnp.sum(S, axis=-1) + inter * jnp.einsum('bhnd,bhntd->bhnt', n_prev, q)
    h = num / jnp.maximum(jnp.abs(den), jnp.exp(-m_t))[..., None]
    return h.reshape(B, H, T, d)

def hybrid_mixer(h, w_in, b_in, conv_w, conv_b, rpb, ml_norm_w, w_out):
    B, T, _ = h.shape
    proj = h @ w_in + b_in
    split_idx = np.cumsum(IN_SPLITS)[:-1].tolist()
    (na_q, na_k, na_v, na_z, ml_q, ml_k, ml_v, ml_o, ml_z,
     i_f, f_f, i_b, f_b) = jnp.split(proj, split_idx, axis=-1)

    na_out = neighbourhood_attention(na_q, na_k, na_v, rpb) * jax.nn.silu(na_z)

    qk = jax.nn.silu(centred_short_conv(jnp.concatenate([ml_q, ml_k], axis=-1), conv_w, conv_b))
    mq, mk = jnp.split(qk, 2, axis=-1)

    def heads(t):
        return t.reshape(B, T, ML_HEADS, ML_HEAD_DIM).transpose(0, 2, 1, 3)

    mq, mk, mv = heads(mq), heads(mk), heads(ml_v)
    i_f, f_f, i_b, f_b = (g.transpose(0, 2, 1) for g in (i_f, f_f, i_b, f_b))
    h_fwd = mlstm_chunkwise(mq, mk, mv, i_f, f_f)
    flip = lambda t: jnp.flip(t, axis=2)
    h_bwd = flip(mlstm_chunkwise(flip(mq), flip(mk), flip(mv), flip(i_b), flip(f_b)))
    hm = (h_fwd + h_bwd).transpose(0, 2, 1, 3) * jax.nn.sigmoid(ml_o).reshape(B, T, ML_HEADS, ML_HEAD_DIM)
    mu = jnp.mean(hm, axis=-1, keepdims=True)
    var = jnp.mean(jnp.square(hm - mu), axis=-1, keepdims=True)
    hm = ((hm - mu) * lax.rsqrt(var + EPS)).reshape(B, T, ML_W) * ml_norm_w
    ml_out = hm * jax.nn.silu(ml_z)

    return jnp.concatenate([na_out, ml_out], axis=-1) @ w_out

def first_inputs(seed: int = 0) -> dict:
    key = jax.random.key(seed)
    ks = jax.random.split(key, 14)
    D = D_MODEL
    x = jax.random.normal(ks[0], (BATCH, SEQ, D), jnp.float32)
    c = jax.random.normal(ks[1], (BATCH, D), jnp.float32)
    w_ada = jax.random.normal(ks[2], (DEPTH, D, 3 * D), jnp.float32) * (0.5 * D ** -0.5)
    b_ada = jax.random.normal(ks[3], (DEPTH, 3 * D), jnp.float32) * 0.02
    norm_w = 1.0 + 0.1 * jax.random.normal(ks[4], (DEPTH, D), jnp.float32)
    w_in = jax.random.normal(ks[5], (DEPTH, D, IN_W), jnp.float32) * (D ** -0.5)
    n_main = 4 * NA_W + 5 * ML_W
    fgate_base = jnp.linspace(3.0, 6.0, ML_HEADS, dtype=jnp.float32)
    gk = jax.random.split(ks[6], 5)
    b_in = jnp.concatenate([
        0.02 * jax.random.normal(gk[0], (DEPTH, n_main), jnp.float32),
        0.1 * jax.random.normal(gk[1], (DEPTH, ML_HEADS), jnp.float32),
        fgate_base + 0.1 * jax.random.normal(gk[2], (DEPTH, ML_HEADS), jnp.float32),
        0.1 * jax.random.normal(gk[3], (DEPTH, ML_HEADS), jnp.float32),
        fgate_base + 0.1 * jax.random.normal(gk[4], (DEPTH, ML_HEADS), jnp.float32),
    ], axis=-1)
    conv_w = jax.random.normal(ks[7], (DEPTH, CONV_W, 2 * ML_W), jnp.float32) * (CONV_W ** -0.5)
    conv_b = 0.02 * jax.random.normal(ks[8], (DEPTH, 2 * ML_W), jnp.float32)
    rpb = 0.1 * jax.random.normal(ks[9], (DEPTH, NA_HEADS, 2 * NA_KH - 1, 2 * NA_KW - 1), jnp.float32)
    ml_norm_w = 1.0 + 0.1 * jax.random.normal(ks[10], (DEPTH, ML_W), jnp.float32)
    w_out = jax.random.normal(ks[11], (DEPTH, MIX_W, D), jnp.float32) * (MIX_W ** -0.5)
    final_norm_w = 1.0 + 0.1 * jax.random.normal(ks[12], (D,), jnp.float32)
    return {'x': x, 'c': c, 'w_ada': w_ada, 'b_ada': b_ada, 'norm_w': norm_w, 'w_in': w_in,
            'b_in': b_in, 'conv_w': conv_w, 'conv_b': conv_b, 'rpb': rpb, 'ml_norm_w': ml_norm_w,
            'w_out': w_out, 'final_norm_w': final_norm_w}

def first_block(x, c, w_ada, b_ada, norm_w, w_in, b_in, conv_w, conv_b, rpb, ml_norm_w, w_out, final_norm_w):
    h_res = x.astype(jnp.float32)
    c_act = jax.nn.silu(c.astype(jnp.float32))
    for l in range(DEPTH):
        mod = c_act @ w_ada[l] + b_ada[l]
        shift, scale, gate = jnp.split(mod, 3, axis=-1)
        h = rmsnorm(h_res, norm_w[l]) * (1.0 + scale[:, None, :]) + shift[:, None, :]
        y = hybrid_mixer(h, w_in[l], b_in[l], conv_w[l], conv_b[l], rpb[l], ml_norm_w[l], w_out[l])
        h_res = h_res + gate[:, None, :] * y
    return rmsnorm(h_res, final_norm_w).astype(x.dtype)


HEAD_DIM = 64
MIX_WIDTH = D_MODEL
FOURIER_WIDTH = MIX_WIDTH // 2
ATTN_WIDTH = MIX_WIDTH - FOURIER_WIDTH
N_FOURIER_GROUPS = FOURIER_WIDTH // HEAD_DIM
N_SLOTS = ATTN_WIDTH // HEAD_DIM
DILATED_CONFIGS = ((128, 1), (512, 4), (2048, 16))
N_CFG = len(DILATED_CONFIGS)
N_ATTN_HEADS = N_SLOTS * N_CFG
QKV_WIDTH = N_ATTN_HEADS * HEAD_DIM
IN_WIDTH = 2 * FOURIER_WIDTH + 3 * QKV_WIDTH + ATTN_WIDTH
SPLIT_POINTS = tuple(int(p) for p in np.cumsum([FOURIER_WIDTH, FOURIER_WIDTH, QKV_WIDTH, QKV_WIDTH, QKV_WIDTH]))
NORM_EPS = 1e-6
MASK_VALUE = -1e30


def alibi_slopes(n):
    return 2.0 ** (-8.0 * jnp.arange(1, n + 1, dtype=jnp.float32) / n)

def rms_norm(t, w):
    t32 = t.astype(jnp.float32)
    return t32 * lax.rsqrt(jnp.mean(t32 * t32, axis=-1, keepdims=True) + NORM_EPS) * w.astype(jnp.float32)

def dilated_window_attention(q, k, v, window, dilation, slopes):
    B, S, H, DH = q.shape
    radius = window // (2 * dilation)
    blk = radius
    L = S // dilation
    N = B * dilation
    nb = -(-L // blk)
    Lp = nb * blk

    def to_sub(t):
        return t.reshape(B, L, dilation, H, DH).transpose(0, 2, 1, 3, 4).reshape(N, L, H, DH)

    qs, ks, vs = to_sub(q), to_sub(k), to_sub(v)
    qb = jnp.pad(qs, ((0, 0), (0, Lp - L), (0, 0), (0, 0))).reshape(N, nb, blk, H, DH)
    pad_kv = ((0, 0), (blk, Lp - L + blk), (0, 0), (0, 0))
    kp = jnp.pad(ks, pad_kv).reshape(N, nb + 2, blk, H, DH)
    vp = jnp.pad(vs, pad_kv).reshape(N, nb + 2, blk, H, DH)
    kb = jnp.concatenate([kp[:, :-2], kp[:, 1:-1], kp[:, 2:]], axis=2)
    vb = jnp.concatenate([vp[:, :-2], vp[:, 1:-1], vp[:, 2:]], axis=2)

    scores = jnp.einsum('nbqhd,nbkhd->nbhqk', qb, kb)
    a = jnp.arange(blk)[:, None]
    c = jnp.arange(3 * blk)[None, :]
    rel = c - blk - a
    key_pos = jnp.arange(nb)[:, None, None] * blk - blk + c[None]
    valid = (jnp.abs(rel)[None] <= radius) & (key_pos >= 0) & (key_pos < L)
    dist = (jnp.abs(rel) * dilation).astype(jnp.float32)
    bias = -slopes[:, None, None] * dist[None]
    scores = jnp.where(valid[None, :, None], scores + bias[None, None], MASK_VALUE)

    m = jnp.max(scores, axis=-1, keepdims=True)
    p = jnp.exp(scores - m)
    s = jnp.sum(p, axis=-1, keepdims=True)
    o = jnp.einsum('nbhqk,nbkhd->nbqhd', p / s, vb)
    lse = (m + jnp.log(s))[..., 0].transpose(0, 1, 3, 2)

    o = o.reshape(N, Lp, H, DH)[:, :L].reshape(B, dilation, L, H, DH).transpose(0, 2, 1, 3, 4).reshape(B, S, H, DH)
    lse = lse.reshape(N, Lp, H)[:, :L].reshape(B, dilation, L, H).transpose(0, 2, 1, 3).reshape(B, S, H)
    return o, lse

def second_inputs(seed: int = 0) -> dict:
    key = jax.random.key(seed)
    ks = jax.random.split(key, 7)
    x = jax.random.normal(ks[0], (BATCH, SEQ, D_MODEL), jnp.float32)
    norm_w = 1.0 + 0.02 * jax.random.normal(ks[1], (D_MODEL,), jnp.float32)
    w_in = jax.random.normal(ks[2], (D_MODEL, IN_WIDTH), jnp.float32) * D_MODEL ** -0.5
    q_norm_w = 1.0 + 0.02 * jax.random.normal(ks[3], (N_ATTN_HEADS, HEAD_DIM), jnp.float32)
    k_norm_w = 1.0 + 0.02 * jax.random.normal(ks[4], (N_ATTN_HEADS, HEAD_DIM), jnp.float32)
    w_fourier = jax.random.normal(ks[5], (N_FOURIER_GROUPS, HEAD_DIM, HEAD_DIM), jnp.float32) * HEAD_DIM ** -0.5
    w_out = jax.random.normal(ks[6], (MIX_WIDTH, D_MODEL), jnp.float32) * MIX_WIDTH ** -0.5
    return {"x": x, "norm_w": norm_w, "w_in": w_in, "q_norm_w": q_norm_w,
            "k_norm_w": k_norm_w, "w_fourier": w_fourier, "w_out": w_out}

def second_block(x, norm_w, w_in, q_norm_w, k_norm_w, w_fourier, w_out):
    B, S, _ = x.shape
    slopes = alibi_slopes(N_SLOTS)
    h = x.astype(jnp.float32)
    for _layer in range(DEPTH):
        hn = rms_norm(h, norm_w)
        proj = hn @ w_in.astype(jnp.float32)
        u_f, g_f, q, k, v, g_a = jnp.split(proj, SPLIT_POINTS, axis=-1)

        u_f = u_f.reshape(B, S, N_FOURIER_GROUPS, HEAD_DIM)
        f = jnp.fft.fft2(u_f, axes=(1, 3), norm="ortho").real.astype(jnp.float32)
        f = jnp.einsum('bsgc,gcd->bsgd', f, w_fourier.astype(jnp.float32)).reshape(B, S, FOURIER_WIDTH)
        y_f = f * jax.nn.silu(g_f)

        q = rms_norm(q.reshape(B, S, N_ATTN_HEADS, HEAD_DIM), q_norm_w) * HEAD_DIM ** -0.5
        k = rms_norm(k.reshape(B, S, N_ATTN_HEADS, HEAD_DIM), k_norm_w)
        v = v.reshape(B, S, N_ATTN_HEADS, HEAD_DIM)
        outs, lses = [], []
        for c, (window, dilation) in enumerate(DILATED_CONFIGS):
            sl = slice(c * N_SLOTS, (c + 1) * N_SLOTS)
            o_c, lse_c = dilated_window_attention(q[:, :, sl], k[:, :, sl], v[:, :, sl], window, dilation, slopes)
            outs.append(o_c)
            lses.append(lse_c)
        alpha = jax.nn.softmax(jnp.stack(lses, axis=0), axis=0)
        o = jnp.sum(alpha[..., None] * jnp.stack(outs, axis=0), axis=0).reshape(B, S, ATTN_WIDTH)
        y_a = o * jax.nn.silu(g_a)

        mixed = jnp.concatenate([y_f, y_a], axis=-1) @ w_out.astype(jnp.float32)
        h = h + mixed
    return h.astype(x.dtype)


def setup_inputs(seed=0):
    out = dict(first_inputs(seed))
    for name, value in second_inputs(seed + 1).items():
        if name != "x":
            out[name + "_2"] = value
    return out


def reference(
    x, c, w_ada, b_ada, norm_w, w_in, b_in, conv_w, conv_b, rpb, ml_norm_w, w_out, final_norm_w,
    norm_w_2, w_in_2, q_norm_w_2, k_norm_w_2, w_fourier_2, w_out_2,
):
    x = first_block(
        x, c, w_ada, b_ada, norm_w, w_in, b_in, conv_w, conv_b, rpb, ml_norm_w, w_out,
        final_norm_w,
    )
    return second_block(
        x, norm_w_2, w_in_2, q_norm_w_2, k_norm_w_2, w_fourier_2, w_out_2,
    )


_drawn_inputs = setup_inputs


def setup_inputs(seed=0):
    import zlib

    import numpy as np

    out = dict(_drawn_inputs(seed))
    spreads = {}
    factors = {'b_ada': 3.652,
     'norm_w': 2.731,
     'conv_b': 8.0,
     'rpb': 8.0,
     'ml_norm_w': 3.635,
     'norm_w_2': 6.355,
     'q_norm_w_2': 8.0,
     'k_norm_w_2': 8.0}
    for name, (base, spread) in spreads.items():
        noise = np.random.default_rng([zlib.crc32(name.encode()), seed]).standard_normal(out[name].shape)
        drawn = base * np.exp(spread * noise) if base else spread * noise
        out[name] = __import__('jax').numpy.asarray(drawn.astype(out[name].dtype))
    for name, factor in factors.items():
        out[name] = (out[name] * factor).astype(out[name].dtype)
    return out
```

```python
from contextlib import ExitStack

import numpy as np

import concourse.bass as bass
from concourse import mybir

F32 = mybir.dt.float32
ALU = mybir.AluOpType
ACT = mybir.ActivationFunctionType

P = 128
T = 2048
D = 1024
KC = D // P
TB = 512
NTB = T // TB
NT = T // P
HALF = D // 2
EPS = 1e-6
BIG = 1e30

GRID_W = 64
ROWS = T // GRID_W
NA_KH = 8
NA_KW = 16
NDY = 2 * NA_KH - 1
NDX = 2 * NA_KW - 1
PAIRS = HALF // P
ML_HEADS = HALF // P
RPB_PAD = 64

DILATIONS = (1, 4, 16)
N_CFG = len(DILATIONS)
QKV = N_CFG * HALF


def open_memory(nc, ctx, sems=None):
    def sb(name, shape, dt=F32):
        return ctx.enter_context(nc.sbuf_tensor(name, shape, dt))

    def ps(name, shape):
        return ctx.enter_context(nc.psum_tensor(name, shape, F32))

    def sem(name):
        made = ctx.enter_context(nc.semaphore(name))
        if sems is not None:
            sems.append(made)
        return made

    return sb, ps, sem


def need(eng, sem, value):
    if value > 0:
        eng.wait_ge(sem, value)


def clear(nc, sems, first):
    ids = sorted(s.num for s in sems[[s.num for s in sems].index(first.num):])
    starts = [i for i in range(len(ids)) if i == 0 or ids[i] != ids[i - 1] + 1] + [len(ids)]
    with nc.Block() as block:
        @block.gpsimd
        def _(pool):
            for i, j in zip(starts, starts[1:]):
                pool.sem_clear(range(ids[i], ids[j - 1] + 1))


def modulate_and_norm(nc, t, hT):
    with ExitStack() as ctx:
        sems = []
        sb, ps, sem = open_memory(nc, ctx, sems)
        ada = sb("ada", [P, 3, KC, TB])
        xg = sb("xg", [P, NTB, 4, D])
        junk = sb("junk0", [P, D])
        ident = sb("ident0", [P, P])
        c_col = sb("c_col", [P, KC])
        c_act = sb("c_act", [P, KC])
        c_rep = sb("c_rep", [P, KC, P])
        b_col = sb("b_col", [P, 2 * KC])
        b_gate = sb("b_gate", [P, D])
        nw = sb("nw", [P, KC])
        gate_b = sb("gate_b", [P, D])
        mod_row = sb("mod_row", [1, 2 * D])
        one = sb("one0", [1, 1])
        mod = sb("mod", [P, 2 * KC])
        gain = sb("gain", [P, KC])
        epst = sb("eps0", [P, 1])
        ssq = sb("ssq0", [P, NT])
        root = sb("root0", [P, NT])
        rstd = sb("rstd0", [P, NT])
        ps_mod = ps("ps_mod", [P, TB])
        ps_gate = ps("ps_gate", [P, 2, TB])
        ps_x = ps("ps_x", [P, 4, TB])
        smalls = sem("m_smalls")
        ada_in = [sem(f"m_ada{i}") for i in range(3)]
        x_in = [sem(f"m_x{i}") for i in range(NTB)]
        ada_used = sem("m_ada_used")
        silu_c = sem("m_silu_c")
        rep_c = sem("m_rep_c")
        gate_out = sem("m_gate_out")
        gate_stored = sem("m_gate_stored")
        row_out = sem("m_row_out")
        mod_turned = sem("m_mod_turned")
        mod_out = sem("m_mod_out")
        gain_out = sem("m_gain_out")
        eps_out = sem("m_eps")
        summed = sem("m_summed")
        rooted = sem("m_rooted")
        recip = sem("m_recip")
        scaled = sem("m_scaled")
        turned = sem("m_turned")
        out_act = sem("m_out_act")
        out_dve = sem("m_out_dve")
        x_v = t["x"].rearrange("a (g j p) d -> p (a g) j d", p=P, j=4)
        w_v = t["w_ada"].rearrange("a (k p) n -> p (a k) n", p=P)
        n_chunks = 3 * D // TB
        with nc.Block() as block:
            @block.sync
            def _(sp):
                sp.dma_start(c_col[:], t["c"].rearrange("a (k p) -> p (a k)", p=P), allow_slow_non_contiguous=True).then_inc(smalls, 16)
                sp.dma_start(b_col[:], t["b_ada"][:, 0:2 * D].rearrange("a (k p) -> p (a k)", p=P), allow_slow_non_contiguous=True).then_inc(smalls, 16)
                sp.dma_start(nw[:], t["norm_w"].rearrange("a (k p) -> p (a k)", p=P), allow_slow_non_contiguous=True).then_inc(smalls, 16)
                sp.dma_start(b_gate[:], t["b_ada"][0, 2 * D:3 * D].partition_broadcast(P)).then_inc(smalls, 16)
                sp.dma_start(ident[:], t["ident"]).then_inc(smalls, 16)
                for j in range(n_chunks):
                    need(sp, ada_used, j - 2)
                    sp.dma_start(ada[:, j % 3], w_v[:, :, j * TB:(j + 1) * TB]).then_inc(ada_in[j % 3], 16)
                need(sp, gate_out, 2)
                sp.dma_start(t["gate_row"], gate_b[0:1, :]).then_inc(gate_stored, 16)
                need(sp, gate_stored, 16)

            @block.scalar
            def _(act):
                need(act, smalls, 80)
                for g in range(NTB):
                    act.dma_start(xg[:, g], x_v[:, g]).then_inc(x_in[g], 16)
                nc.scalar.activation(c_act[:], c_col[:], ACT.Silu).then_inc(silu_c, 1)
                need(act, eps_out, 2)
                for g in range(NTB):
                    need(act, x_in[g], 16)
                    for j in range(4 * g, 4 * g + 4):
                        need(act, summed, j)
                        nc.scalar.activation(junk[:], xg[:, g, j % 4], ACT.Square, accum_out=ssq[:, j:j + 1]).then_inc(summed, 1)
                    need(act, summed, 4 * g + 4)
                    nc.scalar.activation(root[:, 4 * g:4 * g + 4], ssq[:, 4 * g:4 * g + 4], ACT.Sqrt, bias=epst[:, 0:1], scale=1.0 / D).then_inc(rooted, 1)
                need(act, gain_out, 1)
                for g in range(NTB):
                    for k in range(0, KC, 2):
                        need(act, turned, 8 * g + k + 1)
                        nc.scalar.activation(hT[:, k, g * TB:(g + 1) * TB], ps_x[:, k % 4], ACT.Identity,
                                             bias=mod[:, k:k + 1], scale=gain[:, k:k + 1]).then_inc(out_act, 1)

            @block.vector
            def _(dve):
                nc.vector.memset(epst[:], EPS).then_inc(eps_out, 1)
                nc.vector.memset(one[:], 1.0).then_inc(eps_out, 1)
                need(dve, silu_c, 1)
                nc.vector.tensor_copy(c_rep[:], c_act[:, :].unsqueeze(2).broadcast_to([P, KC, P])).then_inc(rep_c, 1)
                for g in range(NTB):
                    need(dve, rooted, g + 1)
                    nc.vector.reciprocal(rstd[:, 4 * g:4 * g + 4], root[:, 4 * g:4 * g + 4]).then_inc(recip, 1)
                    need(dve, recip, g + 1)
                    for j in range(4 * g, 4 * g + 4):
                        nc.vector.tensor_scalar(xg[:, g, j % 4], xg[:, g, j % 4], rstd[:, j:j + 1], None, ALU.mult).then_inc(scaled, 1)
                for j in range(4):
                    need(dve, ada_used, j + 1)
                    nc.vector.tensor_copy(mod_row[:, j * TB:(j + 1) * TB], ps_x[0:1, j]).then_inc(row_out, 1)
                need(dve, smalls, 80)
                need(dve, mod_turned, 1)
                nc.vector.tensor_tensor(mod[:], ps_mod[:, 0:2 * KC], b_col[:], ALU.add).then_inc(mod_out, 1)
                need(dve, mod_out, 1)
                nc.vector.scalar_tensor_tensor(out=gain[:], in0=mod[:, KC:2 * KC], scalar=1.0, in1=nw[:], op0=ALU.add, op1=ALU.mult).then_inc(gain_out, 1)
                need(dve, gain_out, 1)
                for g in range(NTB):
                    for k in range(1, KC, 2):
                        need(dve, turned, 8 * g + k + 1)
                        nc.vector.tensor_scalar(hT[:, k, g * TB:(g + 1) * TB], ps_x[:, k % 4],
                                                gain[:, k:k + 1], mod[:, k:k + 1], ALU.mult, ALU.add).then_inc(out_dve, 1)
                for j in range(2):
                    need(dve, ada_used, 5 + j)
                    nc.vector.tensor_tensor(gate_b[:, j * TB:(j + 1) * TB], ps_gate[:, j], b_gate[:, j * TB:(j + 1) * TB], ALU.add).then_inc(gate_out, 1)

            @block.tensor
            def _(pe):
                def modulation(j):
                    need(pe, ada_in[j % 3], 16 * (j // 3 + 1))
                    if j < 4:
                        for k in range(KC):
                            last = nc.tensor.matmul(ps_x[0:1, j], c_act[:, k:k + 1], ada[:, j % 3, k], start=(k == 0), stop=(k == KC - 1))
                    else:
                        for k in range(KC):
                            last = nc.tensor.matmul(ps_gate[:, j - 4], c_rep[:, k], ada[:, j % 3, k], start=(k == 0), stop=(k == KC - 1))
                    last.then_inc(ada_used, 1)

                need(pe, silu_c, 1)
                need(pe, rep_c, 1)
                for j in range(4):
                    modulation(j)
                need(pe, eps_out, 2)
                need(pe, row_out, 4)
                for m in range(2 * KC):
                    last = nc.tensor.matmul(ps_mod[:, m:m + 1], mod_row[:, m * P:(m + 1) * P], one[:], start=True, stop=True)
                last.then_inc(mod_turned, 1)
                for g in range(NTB):
                    need(pe, scaled, 4 * g + 4)
                    for k in range(KC):
                        n = 8 * g + k - 4
                        if n >= 0:
                            need(pe, out_act if k % 2 == 0 else out_dve, n // 2 + 1)
                        for j in range(4):
                            last = nc.tensor.transpose(ps_x[:, k % 4, j * P:(j + 1) * P], xg[:, g, j, k * P:(k + 1) * P], ident[:])
                        last.then_inc(turned, 1)
                for j in range(4, n_chunks):
                    modulation(j)
        clear(nc, sems, sems[0])


def gate_rows(nc, t, hT, gates, decay):
    with ExitStack() as ctx:
        sems = []
        sb, ps, sem = open_memory(nc, ctx, sems)
        wg = sb("wg", [P, KC, P])
        bg = sb("bg", [P, 1])
        ident = sb("ident1", [P, P])
        pick = sb("pick", [P, 2, P])
        raw = sb("graw", [P, T])
        gi = sb("gi", [36, T])
        gf = sb("gf", [36, T])
        la = sb("la", [36, T])
        lf = sb("lf", [36, T])
        fresh = sb("fresh", [36, T])
        bsum = sb("bsum", [36, T])
        m = sb("mrun", [36, T])
        r = sb("rrow", [36, T])
        m_prev = sb("m_prev", [36, NT])
        rn = fresh
        quant = [sb("quant0", [P, T]), sb("quant1", [P, T])]
        one = sb("one1", [P, 1])
        pg = ps("pg", [P, 4, TB])
        pq = ps("pq", [P, 2, TB])
        pd = ps("pd", [P, 2, TB])
        zero = sb("rpb_zero", [1, RPB_PAD])
        zeroed = sem("g_zeroed")
        padded = sem("g_padded")
        made = sem("g_made")
        cleared = sem("g_cleared")
        loaded = sem("g_loaded")
        proj = sem("g_proj")
        raw_out = sem("g_raw_out")
        d = sem("g_dve")
        a = sem("g_act")
        rows_act = sem("g_rows_act")
        rows_out = sem("g_rows_dve")
        turned = sem("g_turned")
        cols_out = sem("g_cols")
        picked = sem("g_picked")
        stored = sem("g_stored")
        col0 = 9 * HALF
        w_v = t["w_in"].rearrange("a (k p) n -> p (a k) n", p=P)
        with nc.Block() as block:
            @block.sync
            def _(sp):
                sp.dma_start(ident[:], t["ident"]).then_inc(loaded, 16)
                sp.dma_start(pick[:], t["pick"]).then_inc(loaded, 16)
                sp.dma_start(fresh[:], t["fresh"][0, :].partition_broadcast(36)).then_inc(loaded, 16)
                sp.wait_ge(cleared, 2)
                for q in range(4):
                    n = ML_HEADS
                    sp.dma_start(wg[:, :, 32 * q:32 * q + n], w_v[:, :, col0 + n * q:col0 + n * q + n]).then_inc(loaded, 16)
                    sp.dma_start(bg[32 * q:32 * q + n, 0:1], t["b_in"][0, col0 + n * q:col0 + n * q + n].unsqueeze(1)).then_inc(loaded, 16)
                grid_tables(sp, t, zero, zeroed, padded, made)
                sp.wait_ge(rows_out, 2)
                for i in range(2):
                    sp.dma_start(t["r_rows"][i], rn[32 * i:32 * i + ML_HEADS, :]).then_inc(stored, 16)
                sp.wait_ge(stored, 32)
                sp.wait_ge(made, 16 * 2 * PAIRS)

            @block.gpsimd
            def _(pool):
                nc.gpsimd.memset(wg[:], 0.0).then_inc(cleared, 1)
                nc.gpsimd.memset(bg[:], 0.0).then_inc(cleared, 1)
                nc.gpsimd.memset(zero[:], 0.0).then_inc(zeroed, 1)
                nc.gpsimd.memset(gi[:], 0.0).then_inc(cleared, 1)
                nc.gpsimd.memset(gf[:], 0.0).then_inc(cleared, 1)
                nc.gpsimd.memset(quant[0][:], 0.0).then_inc(cleared, 1)
                nc.gpsimd.memset(quant[1][:], 0.0).then_inc(cleared, 1)
                nc.gpsimd.memset(one[:], 1.0).then_inc(cleared, 1)
                nc.gpsimd.memset(m_prev[:], 0.0).then_inc(cleared, 1)

            @block.tensor
            def _(pe):
                pe.wait_ge(loaded, 11 * 16)
                for tb in range(NTB):
                    for k in range(KC):
                        last = nc.tensor.matmul(pg[:, tb], wg[:, k], hT[:, k, tb * TB:(tb + 1) * TB], start=(k == 0), stop=(k == KC - 1))
                    last.then_inc(proj, 1)
                pe.wait_ge(rows_out, 4)
                pe.wait_ge(rows_act, 6)
                for n in range(2 * NT // 4):
                    if n >= 2:
                        pe.wait_ge(cols_out, n - 1)
                    for j in range(4):
                        dr, c = divmod(4 * n + j, NT)
                        last = nc.tensor.transpose(pq[:, n % 2, j * P:(j + 1) * P], quant[dr][:, c * P:(c + 1) * P], ident[:])
                    last.then_inc(turned, 1)
                pe.wait_ge(cols_out, 2 * NT // 4)
                for dr in range(2):
                    nc.tensor.matmul(pd[:, dr, 0:NT * ML_HEADS], pick[:, dr], gates[:, :, dr, 1, :], start=True, stop=True).then_inc(picked, 1)

            @block.scalar
            def _(act):
                act.wait_ge(loaded, 11 * 16)
                act.wait_ge(cleared, 8)
                for tb in range(NTB):
                    act.wait_ge(proj, tb + 1)
                    nc.scalar.activation(raw[:, tb * TB:(tb + 1) * TB], pg[:, tb], ACT.Identity, bias=bg[:, 0:1]).then_inc(raw_out, 1)
                act.wait_ge(d, 4)
                nc.scalar.activation(la[:], gf[:], ACT.Abs).then_inc(a, 1)
                act.wait_ge(a, 1)
                nc.scalar.activation(la[:], la[:], ACT.Exp, scale=-1.0).then_inc(a, 1)
                act.wait_ge(a, 2)
                nc.scalar.activation(la[:], la[:], ACT.Ln, bias=one[0:36, 0:1]).then_inc(a, 1)
                act.wait_ge(d, 12)
                for dr in range(2):
                    way = slice(None) if dr == 0 else slice(None, None, -1)
                    rows = slice(32 * dr, 32 * dr + ML_HEADS)
                    q = quant[dr]
                    nc.scalar.activation(q[32:36, :][:, way], la[rows, :], ACT.Exp).then_inc(rows_act, 1)
                    nc.scalar.activation(q[64:68, :][:, way], m[rows, :], ACT.Exp, scale=-1.0).then_inc(rows_act, 1)
                    nc.scalar.activation(q[96:100, :][:, way], lf[rows, :], ACT.Exp).then_inc(rows_act, 1)

            @block.vector
            def _(dve):
                dve.wait_ge(cleared, 8)
                dve.wait_ge(raw_out, NTB)
                n = ML_HEADS
                nc.vector.tensor_copy(gi[0:n, :], raw[0:n, :]).then_inc(d, 1)
                nc.vector.tensor_copy(gf[0:n, :], raw[32:32 + n, :]).then_inc(d, 1)
                nc.vector.tensor_copy(gi[32:32 + n, :], raw[64:64 + n, ::-1]).then_inc(d, 1)
                nc.vector.tensor_copy(gf[32:32 + n, :], raw[96:96 + n, ::-1]).then_inc(d, 1)
                dve.wait_ge(a, 3)
                dve.wait_ge(d, 4)
                nc.vector.scalar_tensor_tensor(out=lf[:], in0=gf[:], scalar=0.0, in1=la[:], op0=ALU.min, op1=ALU.subtract).then_inc(d, 1)
                dve.wait_ge(loaded, 11 * 16)
                dve.wait_ge(d, 5)
                nc.vector.tensor_tensor_scan(bsum[:], fresh[:], lf[:], 0.0, ALU.mult, ALU.add).then_inc(d, 1)
                nc.vector.tensor_tensor_scan(m[:], lf[:], gi[:], 0.0, ALU.add, ALU.max).then_inc(d, 1)
                dve.wait_ge(d, 7)
                nc.vector.tensor_copy(m_prev[:, 1:NT], m[:, P - 1:T - P:P]).then_inc(d, 1)
                nc.vector.tensor_tensor(r[:], bsum[:], m[:], ALU.subtract).then_inc(d, 1)
                nc.vector.tensor_tensor(gi[:], gi[:], bsum[:], ALU.subtract).then_inc(d, 1)
                dve.wait_ge(d, 10)
                by_chunk = lambda x: x[:, :].rearrange("p (c l) -> p c l", l=P)
                nc.vector.tensor_tensor(by_chunk(la), by_chunk(r), m_prev[:, :].unsqueeze(2).broadcast_to([36, NT, P]), ALU.add).then_inc(d, 1)
                nc.vector.tensor_tensor(by_chunk(lf), by_chunk(gi), r[:, P - 1:T:P].unsqueeze(2).broadcast_to([36, NT, P]), ALU.add).then_inc(d, 1)
                nc.vector.tensor_copy(rn[0:n, :], r[0:n, :]).then_inc(rows_out, 1)
                nc.vector.tensor_copy(rn[32:32 + n, :], r[32:32 + n, ::-1]).then_inc(rows_out, 1)
                nc.vector.tensor_copy(quant[0][0:n, :], gi[0:n, :]).then_inc(rows_out, 1)
                nc.vector.tensor_copy(quant[1][0:n, :], gi[32:32 + n, ::-1]).then_inc(rows_out, 1)
                for k in range(2 * NT // 4):
                    dve.wait_ge(turned, k + 1)
                    dr, c = divmod(4 * k, NT)
                    src = pq[:, k % 2].rearrange("p (c q h) -> p c q h", c=4, q=4)[:, :, :, 0:n]
                    nc.vector.tensor_copy(gates[:, c:c + 4, dr], src).then_inc(cols_out, 1)
                for dr in range(2):
                    dve.wait_ge(picked, dr + 1)
                    nc.vector.tensor_copy(decay[:, dr], pd[:, dr, 0:NT * n].rearrange("p (c h) -> p c h", h=n)).then_inc(d, 1)
        clear(nc, sems, sems[0])


def mlstm(nc, t, hT, mix, gates, decay):
    L = P + 1
    with ExitStack() as ctx:
        sems = []
        sb, ps, sem = open_memory(nc, ctx, sems)
        NW = 5
        K_, Q_, Z_, V_, O_ = range(NW)
        col = {K_: 5, Q_: 4, Z_: 8, V_: 6, O_: 7}
        w = sb("w3", [P, NW - 1, KC, P])
        pre = sb("pre", [P, 2, T + 4])
        kT = sb("kT3", [P, T])
        qT = sb("qT3", [P, T])
        v1 = sb("v1", [P, NT, L])
        og = sb("og", [P, NT, P])
        state = sb("state", [P, NT, 2, L])
        rb = sb("rb", [P, 2, 2, TB])
        kw = sb("kw", [P, 2, 2, P])
        dm = sb("dm", [P, 2, 2, P])
        sd = sb("sd", [P, 2, 2, P])
        hbs = sb("hbs", [P, 2, 2, L])
        hn = sb("hn", [P, 2, 4, 2, L])
        ident = sb("ident3", [P, P])
        causal = sb("causal", [P, 2, P])
        small = sb("small3", [P, ML_HEADS, 18])
        sh = sb("sh3", [P, 18])
        vo_b = sb("vo_b", [P, 2, P])
        gh = sb("gh", [P, NT, 2, 4])
        dh = sb("dh", [P, 2, NT])
        den = sb("den3", [P, 3, 4, 2])
        stats = sb("stats3", [P, NT, 6])
        mv = sb("mv3", [P, NT, 2])
        rs = sb("rs3", [P, 2, NT])
        epst = sb("eps3", [P, 1])
        bank = [ps(f"m{i}", [P, TB]) for i in range(8)]
        consts = sem("l_consts")
        once = sem("l_once")
        w_in = [sem(f"l_w{i}") for i in range(NW)]
        rb_in = [sem("l_rb0"), sem("l_rb1")]
        head_in = sem("l_head_in")
        proj = sem("l_proj")
        out_act = sem("l_out_act")
        out_dve = sem("l_out_dve")
        conv = sem("l_conv")
        soft_k = sem("l_soft_k")
        soft_q = sem("l_soft_q")
        k_ready = sem("l_k_ready")
        o_ready = sem("l_o_ready")
        k_turned = sem("l_k_turned")
        k_weighed = sem("l_k_weighed")
        kv = sem("l_kv")
        carried = sem("l_carried")
        masked = sem("l_masked")
        qk = sem("l_qk")
        decays = sem("l_decays")
        scored = sem("l_scored")
        crossed = sem("l_crossed")
        cross_out = sem("l_cross_out")
        inside = sem("l_inside")
        summed = sem("l_summed")
        dens = sem("l_dens")
        divided = sem("l_divided")
        both = sem("l_both")
        gated = sem("l_gated")
        stat = sem("l_stat")
        rooted = sem("l_rooted")
        normed = sem("l_normed")
        h_turned = sem("l_h_turned")
        h_out = sem("l_h_out")
        stat2 = sem("l_stat2")
        vo_in = sem("l_vo_in")
        w_v = t["w_in"].rearrange("a (k p) n -> p (a k) n", p=P)
        slow = dict(allow_slow_non_contiguous=True)
        n_conv = 5
        with nc.Block() as block:
            @block.sync
            def _(sp):
                rows = [t["b_in"][0, m * HALF:(m + 1) * HALF] for m in range(4, 9)]
                rows += [t["conv_w"][0, j, m * HALF:(m + 1) * HALF] for j in range(n_conv) for m in range(2)]
                rows += [t["conv_b"][0, m * HALF:(m + 1) * HALF] for m in range(2)] + [t["ml_norm_w"][0, :]]
                for n, row in enumerate(rows):
                    sp.dma_start(small[:, :, n], row.rearrange("(h p) -> p h", p=P), **slow).then_inc(consts, 16)
                sp.dma_start(ident[:], t["ident"]).then_inc(consts, 16)
                sp.dma_start(causal[:], t["causal"]).then_inc(consts, 16)
                sp.wait_ge(consts, 24 * 16)

            @block.scalar
            def _(act):
                for s in range(O_):
                    act.dma_start(w[:, s], w_v[:, :, (col[s] + 1) * HALF - P:(col[s] + 1) * HALF]).then_inc(consts, 16)

            @block.gpsimd
            def _(pool):
                nc.gpsimd.memset(pre[:], 0.0).then_inc(once, 1)
                nc.gpsimd.memset(v1[:], 1.0).then_inc(once, 1)
                nc.gpsimd.memset(state[:], 0.0).then_inc(once, 1)
                nc.gpsimd.memset(epst[:], EPS).then_inc(once, 1)

        with nc.Fori(0, ML_HEADS) as back:
            h = (ML_HEADS - 1) - back
            with nc.Block() as block:
                def fetch(sp, b):
                    sp.dma_start(rb[:, b % 2], t["r_rows"][:, bass.ds(h, 1), b * TB:(b + 1) * TB].rearrange("a h n -> h a n")[0].partition_broadcast(P)).then_inc(rb_in[b % 2], 16)

                @block.sync
                def _(sp):
                    sp.dma_start(vo_b[:], t["b_in"][0, 6 * HALF:8 * HALF].rearrange("(m n) -> m n", m=2)[:, bass.ds(h * P, P)].partition_broadcast(P)).then_inc(vo_in, 16)
                    for b in range(2):
                        fetch(sp, b)
                    for s in range(NW):
                        if s == 0:
                            sp.wait_ge(proj, 4)
                            sp.dma_start(w[:, 0], w_v[:, :, bass.ds(h * P + col[O_] * HALF, P)]).then_inc(w_in[O_], 16)
                        else:
                            sp.wait_ge(proj, 4 * s + 4)
                            sp.dma_start(w[:, s % O_], w_v[:, :, bass.ds((ML_HEADS - 2 - back) * P + col[s % O_] * HALF, P)]).then_inc(w_in[s % O_], 16)
                    for b in range(2, NTB):
                        sp.wait_ge(decays, 4 * b - 4)
                        fetch(sp, b)
                    for s in range(O_):
                        sp.wait_ge(w_in[s], 16)

                def combine(pool, h, b):
                    need(pool, divided, b + 1)
                    need(pool, o_ready, 1)
                    nc.gpsimd.tensor_tensor(hn[:, b % 2, :, 0, 0:P], hn[:, b % 2, :, 0, 0:P], hn[:, b % 2, :, 1, 0:P], ALU.add).then_inc(both, 1)
                    need(pool, both, b + 1)
                    nc.gpsimd.tensor_tensor(og[:, 4 * b:4 * b + 4], og[:, 4 * b:4 * b + 4], hn[:, b % 2, :, 0, 0:P], ALU.mult).then_inc(gated, 1)

                @block.gpsimd
                def _(pool):
                    nc.gpsimd.tensor_copy(sh[:], small[:, bass.ds(h, 1)][:, 0]).then_inc(head_in, 1)
                    nc.gpsimd.tensor_copy(gh[:], gates[:, :, :, :, bass.ds(h, 1)][:, :, :, :, 0]).then_inc(head_in, 1)
                    nc.gpsimd.tensor_copy(dh[:], decay[:, :, :, bass.ds(h, 1)][:, :, :, 0]).then_inc(head_in, 1)

                    for b in range(NTB):
                        need(pool, rb_in[b % 2], 16 * (b // 2) + 16)
                        view = rb[:, b % 2].rearrange("p d (c l) -> p d c l", l=P)
                        for dr in range(2):
                            nc.gpsimd.tensor_tensor(view[:, dr], view[:, dr], causal[:, dr].unsqueeze(1).broadcast_to([P, 4, P]), ALU.add).then_inc(masked, 1)
                        if b >= 1:
                            combine(pool, h, b - 1)
                    combine(pool, h, NTB - 1)

                @block.tensor
                def _(pe):
                    for n in range(20):
                        s = n // 4
                        if n == 16:
                            pe.wait_ge(w_in[O_], 16)
                        if 2 <= n < 14:
                            need(pe, out_act, n - 1)
                        elif n >= 14:
                            need(pe, out_dve, n - 13)
                        if s < V_:
                            for k in range(KC):
                                last = nc.tensor.matmul(bank[n % 2][:], w[:, s % O_, k], hT[:, k, (n % 4) * TB:(n % 4 + 1) * TB], start=(k == 0), stop=(k == KC - 1))
                        else:
                            for j in range(4):
                                c = 4 * (n % 4) + j
                                for k in range(KC):
                                    last = nc.tensor.matmul(bank[n % 2][:, j * P:(j + 1) * P], hT[:, k, c * P:(c + 1) * P], w[:, s % O_, k], start=(k == 0), stop=(k == KC - 1))
                        last.then_inc(proj, 1)
                    NS = NT - 1

                    def turn(i):
                        if i >= 2:
                            need(pe, k_weighed, 2 * i - 2)
                        for dr, c in ((0, i), (1, NT - 1 - i)):
                            last = nc.tensor.transpose(bank[2 + i % 2][:, dr * P:(dr + 1) * P], kT[:, c * P:(c + 1) * P], ident[:])
                        last.then_inc(k_turned, 1)

                    need(pe, k_ready, 1)
                    turn(0)
                    for i in range(NS):
                        if i + 1 < NS:
                            turn(i + 1)
                        need(pe, k_weighed, 2 * i + 2)
                        if i == 0:
                            need(pe, out_dve, 4)
                        if i >= 2:
                            need(pe, carried, 2 * i - 2)
                        for dr, c in ((0, i), (1, NT - 1 - i)):
                            last = nc.tensor.matmul(bank[4 + i % 2][:, dr * L:(dr + 1) * L], kw[:, i % 2, dr], v1[:, c], start=True, stop=True)
                        last.then_inc(kv, 1)

                    def scores(c):
                        if c >= 2:
                            need(pe, scored, c - 1)
                        nc.tensor.matmul(bank[2 + c % 2][:, 0:P], kT[:, c * P:(c + 1) * P], qT[:, c * P:(c + 1) * P], start=True, stop=True).then_inc(qk, 1)

                    need(pe, soft_q, 1)
                    need(pe, k_weighed, 2 * NS)
                    scores(0)
                    need(pe, carried, 2 * NS)
                    for c in range(NT):
                        if c + 1 < NT:
                            scores(c + 1)
                        if c >= 2:
                            need(pe, cross_out, 2 * c - 2)
                        nc.tensor.matmul(bank[4 + c % 2][:, 0:2 * L], qT[:, c * P:(c + 1) * P], state[:, c].rearrange("p d l -> p (d l)"), start=True, stop=True).then_inc(crossed, 1)
                        need(pe, scored, c + 1)
                        need(pe, summed, max(c - 1, 0))
                        for dr in range(2):
                            last = nc.tensor.matmul(bank[6 + c % 2][:, dr * L:(dr + 1) * L], sd[:, c % 2, dr], v1[:, c], start=True, stop=True)
                        last.then_inc(inside, 1)
                    for b in range(NTB):
                        need(pe, normed, 4 * b + 4)
                        if b < 2:
                            need(pe, out_dve, 8)
                        else:
                            need(pe, h_out, b - 1)
                        for j in range(4):
                            last = nc.tensor.transpose(bank[b % 2][:, j * P:(j + 1) * P], og[:, 4 * b + j], ident[:])
                        last.then_inc(h_turned, 1)

                @block.scalar
                def _(act):
                    need(act, head_in, 3)
                    for n in range(12):
                        s = n // 4
                        need(act, proj, n + 1)
                        b = slice((n % 4) * TB, (n % 4 + 1) * TB)
                        if s == K_ or s == Q_:
                            dst, bc = pre[:, s, 2 + b.start:2 + b.stop], (1 if s == K_ else 0)
                            nc.scalar.activation(dst, bank[n % 2][:], ACT.Identity, bias=sh[:, bc:bc + 1]).then_inc(out_act, 1)
                        else:
                            nc.scalar.activation(mix[:, bass.ds(h, 1), b][:, 0], bank[n % 2][:], ACT.Silu, bias=sh[:, 4:5]).then_inc(out_act, 1)
                    need(act, conv, n_conv)
                    nc.scalar.activation(kT[:], kT[:], ACT.Silu, bias=sh[:, 16:17]).then_inc(soft_k, 1)
                    need(act, conv, 2 * n_conv)
                    nc.scalar.activation(qT[:], qT[:], ACT.Silu, bias=sh[:, 15:16]).then_inc(soft_q, 1)
                    need(act, out_dve, 8)
                    nc.scalar.activation(og[:], og[:], ACT.Sigmoid).then_inc(o_ready, 1)
                    NS = NT - 1
                    for i in range(NS):
                        need(act, k_turned, i + 1)
                        need(act, kv, max(i - 1, 0))
                        for dr, c in ((0, i), (1, NT - 1 - i)):
                            nc.scalar.activation(kw[:, i % 2, dr], bank[2 + i % 2][:, dr * P:(dr + 1) * P], ACT.Identity,
                                                 scale=gh[:, c, dr, 3:4]).then_inc(k_weighed, 1)

                    def exps(c):
                        need(act, masked, 2 * (c // 4) + 2)
                        need(act, scored, max(c - 1, 0))
                        for dr in range(2):
                            x = nc.scalar.activation(dm[:, c % 2, dr], rb[:, (c // 4) % 2, dr, (c % 4) * P:(c % 4 + 1) * P], ACT.Exp, bias=gh[:, c, dr, 0:1])
                        x.then_inc(decays, 1)

                    exps(0)
                    for c in range(NT):
                        if c + 1 < NT:
                            exps(c + 1)
                        need(act, crossed, c + 1)
                        need(act, summed, max(c - 1, 0))
                        for dr in range(2):
                            nc.scalar.activation(hbs[:, c % 2, dr], bank[4 + c % 2][:, dr * L:(dr + 1) * L], ACT.Identity,
                                                 scale=gh[:, c, dr, 1:2]).then_inc(cross_out, 1)
                    need(act, stat, 2 * NT)
                    nc.scalar.activation(rs[:, 0], mv[:, :, 1], ACT.Sqrt, bias=epst[:, 0:1]).then_inc(rooted, 1)

                @block.vector
                def _(dve):
                    need(dve, head_in, 3)
                    for s, dst in ((K_, kT), (Q_, qT)):
                        need(dve, out_act, 4 * s + 4)
                        src = 1 if s == K_ else 0
                        for j in range(n_conv):
                            wj = sh[:, 5 + 2 * j + src:6 + 2 * j + src]
                            if j == 0:
                                x = nc.vector.tensor_scalar(dst[:], pre[:, s, 0:T], wj, None, ALU.mult)
                            else:
                                need(dve, conv, s * n_conv + j)
                                x = nc.vector.scalar_tensor_tensor(out=dst[:], in0=pre[:, s, j:j + T], scalar=wj, in1=dst[:], op0=ALU.mult, op1=ALU.add)
                            x.then_inc(conv, 1)
                    need(dve, vo_in, 16)
                    for n in range(12, 20):
                        s = n // 4
                        need(dve, proj, n + 1)
                        if n == 16:
                            need(dve, soft_k, 1)
                            nc.vector.tensor_scalar(kT[:], kT[:], float(P) ** -0.5, None, ALU.mult).then_inc(k_ready, 1)
                        dst = v1[:, 4 * (n % 4):4 * (n % 4) + 4, 0:P] if s == V_ else og[:, 4 * (n % 4):4 * (n % 4) + 4]
                        bias = vo_b[:, s - V_].unsqueeze(1).broadcast_to([P, 4, P])
                        nc.vector.tensor_tensor(dst, bank[n % 2][:, :].rearrange("p (c l) -> p c l", l=P), bias, ALU.add).then_inc(out_dve, 1)
                    NS = NT - 1
                    for i in range(NS):
                        need(dve, kv, i + 1)
                        if i > 0:
                            need(dve, carried, 2 * i)
                        for dr, c, nxt in ((0, i, i + 1), (1, NT - 1 - i, NT - 2 - i)):
                            nc.vector.scalar_tensor_tensor(out=state[:, nxt, dr], in0=state[:, c, dr], scalar=dh[:, dr, c:c + 1],
                                                           in1=bank[4 + i % 2][:, dr * L:(dr + 1) * L], op0=ALU.mult, op1=ALU.add).then_inc(carried, 1)

                    def score(c):
                        need(dve, qk, c + 1)
                        need(dve, decays, c + 1)
                        need(dve, inside, max(c - 1, 0))
                        nc.vector.tensor_tensor(sd[:, c % 2], bank[2 + c % 2][:, 0:P].unsqueeze(1).broadcast_to([P, 2, P]), dm[:, c % 2], ALU.mult).then_inc(scored, 1)

                    def moments(g):
                        need(dve, gated, g + 1)
                        for c in range(4 * g, 4 * g + 4):
                            nc.vector.bn_stats(stats[:, c], og[:, c]).then_inc(stat, 1)
                        need(dve, stat, 8 * g + 4)
                        for c in range(4 * g, 4 * g + 4):
                            nc.vector.bn_aggr(mv[:, c], stats[:, c]).then_inc(stat, 1)

                    score(0)
                    for c in range(NT):
                        if c + 1 < NT:
                            score(c + 1)
                        if c >= 6 and c % 4 == 2:
                            moments(c // 4 - 1)
                        g, j = divmod(c, 4)
                        need(dve, inside, c + 1)
                        need(dve, cross_out, 2 * c + 2)
                        if j == 0:
                            need(dve, gated, max(g - 1, 0))
                        nc.vector.tensor_tensor(hn[:, g % 2, j], bank[6 + c % 2][:, 0:2 * L].rearrange("p (d l) -> p d l", l=L), hbs[:, c % 2], ALU.add).then_inc(summed, 1)
                        if j == 3:
                            need(dve, summed, c + 1)
                            raw = hn[:, g % 2, :, :, P]
                            n0 = 3 * g
                            nc.vector.scalar_tensor_tensor(out=den[:, 0], in0=raw, scalar=-1.0, in1=raw, op0=ALU.mult, op1=ALU.max).then_inc(dens, 1)
                            need(dve, dens, n0 + 1)
                            nc.vector.tensor_tensor(den[:, 1], den[:, 0], gh[:, 4 * g:4 * g + 4, :, 2], ALU.max).then_inc(dens, 1)
                            need(dve, dens, n0 + 2)
                            nc.vector.reciprocal(den[:, 2], den[:, 1]).then_inc(dens, 1)
                            need(dve, dens, n0 + 3)
                            body = hn[:, g % 2].rearrange("p c d l -> p (c d) l")[:, :, 0:P]
                            nc.vector.tensor_tensor(body, body, den[:, 2].rearrange("p c d -> p (c d)").unsqueeze(2).broadcast_to([P, 8, P]), ALU.mult).then_inc(divided, 1)
                    moments(NTB - 1)
                    need(dve, rooted, 1)
                    nc.vector.reciprocal(rs[:, 1], rs[:, 0]).then_inc(stat2, 1)
                    need(dve, stat2, 1)
                    for c in range(NT):
                        nc.vector.tensor_scalar(og[:, c], og[:, c], mv[:, c, 0:1], rs[:, 1, c:c + 1], ALU.subtract, ALU.mult).then_inc(normed, 1)
                    for b in range(NTB):
                        need(dve, h_turned, b + 1)
                        m = mix[:, bass.ds(h, 1), b * TB:(b + 1) * TB][:, 0]
                        nc.vector.scalar_tensor_tensor(out=m, in0=bank[b % 2][:], scalar=sh[:, 17:18], in1=m, op0=ALU.mult, op1=ALU.mult).then_inc(h_out, 1)
            clear(nc, sems, w_in[0])
        clear(nc, sems, sems[0])


class Attend:

    def __init__(self, nc, ctx, sems, tag, keys, width, p_bufs, units):
        sb, ps, sem = open_memory(nc, ctx, sems)
        self.units = units
        self.p_bufs = p_bufs
        self.sneg = sb(tag + "_sneg", [P, 2, keys])
        self.p = sb(tag + "_p", [P, p_bufs, width])
        self.pt = sb(tag + "_pt", [P, 2, width])
        self.negmax = sb(tag + "_negmax", [P, units])
        self.total = sb(tag + "_total", [P, units])
        self.inverse = sb(tag + "_inverse", [P, units])
        self.qk = sem(tag + "_qk")
        self.biased = sem(tag + "_biased")
        self.exped = sem(tag + "_exped")
        self.inverted = sem(tag + "_inverted")
        self.normed = sem(tag + "_normed")
        self.turned = sem(tag + "_turned")
        self.turned_out = sem(tag + "_turned_out")
        self.pv = sem(tag + "_pv")
        self.out = sem(tag + "_out")



def grid_units():
    units = []
    for r in range(ROWS):
        start = min(max(r - NA_KH // 2, 0), ROWS - NA_KH)
        at, wide = start * GRID_W, NA_KH * GRID_W
        if start % 2:
            pieces = [(at + wide - GRID_W, GRID_W, 0), (at, wide - GRID_W, GRID_W)]
            c = start // 2
            chunks = [(0, NT + c)] + [(j, c + j) for j in range(1, 4)]
        else:
            pieces = [(at, wide, 0)]
            chunks = [(j, start // 2 + j) for j in range(4)]
        units.append((r, pieces, 0, wide, chunks, start - r + NA_KH - 1, start % 2))
    return units


def attend_pe(nc, pe, at, units, u0, bank, qbd, kT, vals, ident):
    n = len(units)

    def scores(i):
        u = u0 + i
        need(pe, at.biased, max(u - 3, 0))
        q, pieces = units[i][0], units[i][1]
        for k0, w, c0 in pieces:
            last = nc.tensor.matmul(bank[u % 4][:, c0:c0 + w], qbd[:, q], kT[:, k0:k0 + w], start=True, stop=True)
        last.then_inc(at.qk, 1)

    def turn(i):
        u = u0 + i
        need(pe, at.normed, u + 1)
        need(pe, at.turned_out, max(u - 1, 0))
        for j, _ in units[i][4]:
            last = nc.tensor.transpose(bank[4 + u % 2][:, j * P:(j + 1) * P], at.p[:, u % at.p_bufs, j * P:(j + 1) * P], ident[:])
        last.then_inc(at.turned, 1)

    def values(i):
        u = u0 + i
        need(pe, at.turned_out, u + 1)
        if u % 4 == 0:
            need(pe, at.out, 2 * max(u // 4 - 1, 0))
        chunks = units[i][4]
        for m, (j, c) in enumerate(chunks):
            last = nc.tensor.matmul(bank[6 + (u // 4) % 2][:, (u % 4) * P:(u % 4 + 1) * P], vals[:, c], at.pt[:, u % 2, j * P:(j + 1) * P],
                                    start=(m == 0), stop=(m == len(chunks) - 1))
        last.then_inc(at.pv, 1)

    for i in range(3):
        scores(i)
    for i in range(n):
        if i + 3 < n:
            scores(i + 3)
        turn(i)
        if i >= 1:
            values(i - 1)
    values(n - 1)


def attend_act(nc, act, at, units, u0, bank, turned_out=True):
    n = len(units)

    def exps(i):
        u = u0 + i
        off, w = units[i][2], units[i][3]
        need(act, at.biased, u + 1)
        need(act, at.turned, max(u - at.p_bufs + 1, 0))
        nc.scalar.activation(at.p[:, u % at.p_bufs, off:off + w], at.sneg[:, u % 2, 0:w], ACT.Exp,
                             bias=at.negmax[:, u:u + 1], scale=-1.0, accum_out=at.total[:, u:u + 1]).then_inc(at.exped, 1)

    exps(0)
    exps(1)
    for i in range(n):
        if i + 2 < n:
            exps(i + 2)
        if turned_out:
            copy_turned(nc, act, nc.scalar.copy, at, units, u0, bank, i)


def copy_turned(nc, eng, copy, at, units, u0, bank, i):
    u = u0 + i
    chunks = units[i][4]
    j0, j1 = chunks[0][0], chunks[-1][0] + 1
    need(eng, at.turned, u + 1)
    need(eng, at.pv, max(u - 1, 0))
    copy(at.pt[:, u % 2, j0 * P:j1 * P], bank[4 + u % 2][:, j0 * P:j1 * P]).then_inc(at.turned_out, 1)


def attend_pool(nc, pool, at, units, u0):
    for i, unit in enumerate(units):
        u = u0 + i
        off, w = unit[2], unit[3]
        p = at.p[:, u % at.p_bufs, off:off + w]
        need(pool, at.inverted, u + 1)
        nc.gpsimd.tensor_scalar(p, p, at.inverse[:, u:u + 1], None, ALU.mult).then_inc(at.normed, 1)


def attend_dve(nc, dve, at, units, u0, bank, bias_of, write_out, turned_out=False):
    n = len(units)

    def bias(i):
        u = u0 + i
        w = units[i][3]
        need(dve, at.qk, u + 1)
        need(dve, at.exped, max(u - 1, 0))
        nc.vector.tensor_tensor_reduce(out=at.sneg[:, u % 2, 0:w], in0=bank[u % 4][:, 0:w], in1=bias_of(units[i]), scale=1.0,
                                       scalar=3.0e38, op0=ALU.add, op1=ALU.min, accum_out=at.negmax[:, u:u + 1]).then_inc(at.biased, 1)

    def invert(i):
        u = u0 + i
        need(dve, at.exped, u + 1)
        nc.vector.reciprocal(at.inverse[:, u:u + 1], at.total[:, u:u + 1]).then_inc(at.inverted, 1)

    bias(0)
    bias(1)
    invert(0)
    for i in range(n):
        if i + 2 < n:
            bias(i + 2)
        if i + 1 < n:
            invert(i + 1)
        if turned_out:
            copy_turned(nc, dve, nc.vector.tensor_copy, at, units, u0, bank, i)
        if i % 4 == 1 and i >= 5:
            write_out((u0 + i - 5) // 4)
    write_out((u0 + n) // 4 - 1)


def grid_tables(sp, t, zero, zeroed, padded, made):
    flat = 2 * PAIRS * NDY * NDX
    pad = t["rpb_pad"]
    need(sp, zeroed, 1)
    sp.dma_start(pad[0:1, 0:RPB_PAD], zero[:]).then_inc(padded, 16)
    sp.dma_start(pad[0:1, RPB_PAD + flat:2 * RPB_PAD + flat], zero[:]).then_inc(padded, 16)
    sp.dma_start(pad[0:1, RPB_PAD:RPB_PAD + flat], t["rpb"].rearrange("a h y x -> a (h y x)")).then_inc(padded, 16)
    need(sp, padded, 48)
    for h in range(2 * PAIRS):
        at = RPB_PAD + h * NDY * NDX + NA_KW - 1
        src = bass.AP(tensor=pad.tensor, offset=at, ap=[[NDX, NDY], [-1, GRID_W], [1, GRID_W]])
        sp.dma_start(t["rpb_rows"][h // 2, h % 2].rearrange("q y k -> y q k"), src).then_inc(made, 16)


def grid_attention(nc, t, hT, mix):
    units = grid_units()
    NU = len(units)
    with ExitStack() as ctx:
        sems = []
        sb, ps, sem = open_memory(nc, ctx, sems)
        consts = sem("n_consts")
        once = sem("n_once")
        first = sem("n_table_in")
        table_in = first
        at = Attend(nc, ctx, sems, "na", NA_KH * GRID_W, NA_KH * GRID_W, 3, NU)
        K_, Q_, Z_, V_ = range(4)
        col = {K_: 1, Q_: 0, Z_: 3, V_: 2}
        n_wrap = (ROWS - NA_KH) // 2
        w = sb("w1", [P, 4, KC, P])
        kT = sb("kT1", [P, T])
        qbd = sb("qbd1", [P, NU, P])
        vals = sb("vals1", [P, NT + n_wrap, P])
        table = sb("table1", [P, NDY, GRID_W])
        odd = sb("odd1", [P, NA_KH, GRID_W])
        mask = sb("mask1", [P, GRID_W])
        ident = sb("ident_na", [P, P])
        small = sb("small1", [P, 4, PAIRS])
        v_b = sb("v_b1", [P, HALF])
        bank = [ps(f"n{i}", [P, TB]) for i in range(8)]
        w_in = [sem(f"n_w{i}") for i in range(4)]
        tables = sem("n_tables")
        wrapped = sem("n_wrapped")
        proj = sem("n_proj")
        out_act = sem("n_out_act")
        out_dve = sem("n_out_dve")
        w_v = t["w_in"].rearrange("a (k p) n -> p (a k) n", p=P)
        scale = float(GRID_W) ** -0.5
        assert GRID_W == P // 2
        with nc.Block() as block:
            @block.sync
            def _(sp):
                for m in range(4):
                    sp.dma_start(small[:, m], t["b_in"][0, m * HALF:(m + 1) * HALF].rearrange("(h p) -> p h", p=P), allow_slow_non_contiguous=True).then_inc(consts, 16)
                sp.dma_start(v_b[:], t["b_in"][0, 2 * HALF:3 * HALF].partition_broadcast(P)).then_inc(consts, 16)
                sp.dma_start(ident[:], t["ident"]).then_inc(consts, 16)
                sp.dma_start(mask[:], t["na_mask"]).then_inc(consts, 16)
                for s in range(4):
                    sp.dma_start(w[:, s], w_v[:, :, col[s] * HALF:col[s] * HALF + P]).then_inc(consts, 16)
                sp.wait_ge(consts, 11 * 16)

            @block.gpsimd
            def _(pool):
                nc.gpsimd.memset(qbd[:], 0.0).then_inc(once, 1)

            @block.vector
            def _(dve):
                dve.wait_ge(consts, 11 * 16)
                nc.vector.tensor_scalar(small[:, 0], small[:, 0], -scale, None, ALU.mult).then_inc(once, 1)

        with nc.Fori(0, PAIRS) as g:
            with nc.Block() as block:
                @block.sync
                def _(sp):
                    sp.dma_start(table[:], t["rpb_rows"][bass.ds(g, 1)].rearrange("a h q y k -> (a h q) y k")).then_inc(table_in, 16)
                    for s in range(4):
                        sp.wait_ge(proj, 4 * s + 4)
                        sp.dma_start(w[:, s], w_v[:, :, bass.ds((g + 1) * P + col[s] * HALF, P)]).then_inc(w_in[s], 16)
                    for s in range(4):
                        sp.wait_ge(w_in[s], 16)

                @block.gpsimd
                def _(pool):
                    need(pool, table_in, 16)
                    nc.gpsimd.tensor_tensor(table[:], mask[:, :].unsqueeze(1).broadcast_to([P, NDY, GRID_W]), table[:], ALU.subtract).then_inc(tables, 1)
                    need(pool, tables, 1)
                    d0 = NA_KH // 2 - 1
                    nc.gpsimd.tensor_copy(odd[:, 0], table[:, d0 + NA_KH - 1]).then_inc(tables, 1)
                    nc.gpsimd.tensor_copy(odd[:, 1:NA_KH], table[:, d0:d0 + NA_KH - 1]).then_inc(tables, 1)
                    need(pool, tables, 3)
                    need(pool, out_dve, 4)
                    h = P // 2
                    nc.gpsimd.tensor_copy(vals[0:h, NT:], vals[0:h, 4:4 + n_wrap]).then_inc(wrapped, 1)
                    nc.gpsimd.tensor_copy(vals[h:P, NT:], vals[h:P, 0:n_wrap]).then_inc(wrapped, 1)
                    attend_pool(nc, pool, at, units, 0)

                @block.tensor
                def _(pe):
                    for n in range(16):
                        s = n // 4
                        need(pe, out_act, n - 3)
                        for k in range(KC):
                            tb = n % 4
                            if s < V_:
                                last = nc.tensor.matmul(bank[n % 4][:], w[:, s, k], hT[:, k, tb * TB:(tb + 1) * TB], start=(k == 0), stop=(k == KC - 1))
                        if s == V_:
                            for j in range(4):
                                c = 4 * tb + j
                                for k in range(KC):
                                    last = nc.tensor.matmul(bank[n % 4][:, j * P:(j + 1) * P], hT[:, k, c * P:(c + 1) * P], w[:, s, k], start=(k == 0), stop=(k == KC - 1))
                        last.then_inc(proj, 1)
                    need(pe, out_dve, 4)
                    need(pe, wrapped, 2)
                    attend_pe(nc, pe, at, units, 0, bank, qbd, kT, vals, ident)

                @block.scalar
                def _(act):
                    for n in range(12):
                        s, tb = divmod(n, 4)
                        need(act, proj, n + 1)
                        b = slice(tb * TB, (tb + 1) * TB)
                        if s == K_:
                            x = nc.scalar.activation(kT[:, b], bank[n % 4][:], ACT.Identity, bias=small[:, 1, bass.ds(g, 1)])
                        elif s == Q_:
                            for h in range(2):
                                rows = slice(h * GRID_W, (h + 1) * GRID_W)
                                x = nc.scalar.activation(qbd[rows, 8 * tb:8 * tb + 8, h * GRID_W:(h + 1) * GRID_W], bank[n % 4][rows, :].rearrange("p (b q) -> p b q", q=GRID_W),
                                                         ACT.Identity, bias=small[rows, 0, bass.ds(g, 1)], scale=-scale)
                        else:
                            x = nc.scalar.activation(mix[:, bass.ds(g, 1), b][:, 0], bank[n % 4][:], ACT.Silu, bias=small[:, 3, bass.ds(g, 1)])
                        x.then_inc(out_act, 1)
                    attend_act(nc, act, at, units, 0, bank)

                @block.vector
                def _(dve):
                    for tb in range(NTB):
                        need(dve, proj, 12 + tb + 1)
                        bias = v_b[:, bass.ds(g * P, P)].unsqueeze(1).broadcast_to([P, 4, P])
                        nc.vector.tensor_tensor(vals[:, 4 * tb:4 * tb + 4], bank[tb][:, :].rearrange("p (c l) -> p c l", l=P), bias, ALU.add).then_inc(out_dve, 1)
                    need(dve, tables, 3)

                    def bias_of(unit):
                        return (odd[:] if unit[6] else table[:, unit[5]:unit[5] + NA_KH]).rearrange("p y k -> p (y k)")

                    def write_out(b):
                        need(dve, at.pv, 4 * b + 4)
                        for h in range(2):
                            rows = slice(h * GRID_W, (h + 1) * GRID_W)
                            m = mix[rows, bass.ds(g, 1), 4 * b * GRID_W:4 * (b + 1) * GRID_W][:, 0].rearrange("p (u q) -> p u q", q=GRID_W)
                            src = bank[6 + b % 2][rows, :].rearrange("p (u q) -> p u q", q=P)[:, :, h * GRID_W:(h + 1) * GRID_W]
                            nc.vector.tensor_tensor(m, src, m, ALU.mult).then_inc(at.out, 1)

                    attend_dve(nc, dve, at, units, 0, bank, bias_of, write_out)
            clear(nc, sems, first)
        clear(nc, sems, sems[0])


def project_out(nc, t, halves, gated, hT2):
    tag = "a" if gated else "z"
    R = NT // 2
    w_src = t["w_out"].rearrange("a (k p) n -> p (a k) n", p=P) if gated else t["w_out_2"].rearrange("(k p) n -> p k n", p=P)
    x_src = (t["x"][0] if gated else t["x1"]).rearrange("(i b p) d -> i b p d", p=P, b=R)
    y_dst = (t["x1"] if gated else t["out"][0]).rearrange("(i b p) d -> i b p d", p=P, b=R)
    with ExitStack() as ctx:
        sems = []
        sb, ps, sem = open_memory(nc, ctx, sems)
        w = sb(tag + "_w", [P, KC, D])
        x = sb(tag + "_x", [P, 2, D])
        stage = sb(tag + "_stage", [P, 2, KC, P])
        y = sb(tag + "_y", [P, 2, D])
        consts = sem(tag + "_consts")
        w_in = [sem(f"{tag}_w_in{k}") for k in range(KC)]
        if gated:
            xs = sb("a_xs", [P, 2, D])
            gate_b = sb("a_gate", [P, D])
            fw_b = sb("a_fw", [P, D])
            nw = sb("a_nw", [P, KC])
            ident = sb("a_ident", [P, P])
            epst = sb("a_eps", [P, 1])
            st = sb("a_st", [P, R, 6])
            once = sem("a_once")
            ys = sem("a_ys")
            squared = sem("a_squared")
            rooted = sem("a_rooted")
            recip = sem("a_recip")
            normed = sem("a_normed")
            scaled = sem("a_scaled")
            turned = sem("a_turned")
            out = sem("a_out")
            first = ys
        x_in = [sem(tag + "_x_in0"), sem(tag + "_x_in1")]
        if not gated:
            first = x_in[0]
        staged = sem(tag + "_staged")
        proj = sem(tag + "_proj")
        added = sem(tag + "_added")
        stored = [sem(tag + "_stored0"), sem(tag + "_stored1")]
        bank = [ps(f"{tag}{i}", [P, TB]) for i in range(8)]
        with nc.Block() as block:
            @block.sync
            def _(sp):
                for k in range(KC):
                    sp.dma_start(w[:, k], w_src[:, k]).then_inc(w_in[k], 16)
                if gated:
                    sp.dma_start(gate_b[:], t["gate_row"][0, :].partition_broadcast(P)).then_inc(consts, 16)
                    sp.dma_start(fw_b[:], t["final_norm_w"].partition_broadcast(P)).then_inc(consts, 16)
                    sp.dma_start(nw[:], t["norm_w_2"].rearrange("(k p) -> p k", p=P), allow_slow_non_contiguous=True).then_inc(consts, 16)
                    sp.dma_start(ident[:], t["ident"]).then_inc(consts, 16)

            if gated:
                @block.vector
                def _(dve):
                    nc.vector.memset(epst[:], EPS).then_inc(once, 1)

        with nc.Fori(0, NT // R) as i:
            with nc.Block() as block:
                @block.sync
                def _(sp):
                    def load(b):
                        sp.dma_start(x[:, b % 2], x_src[bass.ds(i, 1), b].rearrange("i p d -> (i p) d")).then_inc(x_in[b % 2], 16)

                    load(0)
                    load(1)
                    for b in range(R):
                        if gated:
                            sp.wait_ge(normed, b + 1)
                        sp.wait_ge(added, b + 1 if gated else 2 * b + 2)
                        sp.dma_start(y_dst[bass.ds(i, 1), b].rearrange("i p d -> (i p) d"), y[:, b % 2]).then_inc(stored[b % 2], 16)
                        if b + 2 < R:
                            load(b + 2)
                    for s in stored:
                        sp.wait_ge(s, 16 * R // 2)

                @block.gpsimd
                def _(pool):
                    def stage_in(b):
                        need(pool, proj, 2 * (b - 1))
                        for n, half in enumerate(halves):
                            nc.gpsimd.tensor_copy(stage[:, b % 2, 4 * n:4 * n + 4], half[:, :, bass.ds(i * R * P + b * P, P)]).then_inc(staged, 1)

                    stage_in(0)
                    stage_in(1)
                    for b in range(R):
                        if b + 2 < R:
                            stage_in(b + 2)
                        if gated:
                            pool.wait_ge(ys, 2 * b + 2)
                            pool.wait_ge(x_in[b % 2], 16 * (b // 2 + 1))
                            nc.gpsimd.tensor_tensor(y[:, b % 2], y[:, b % 2], x[:, b % 2], ALU.add).then_inc(added, 1)

                @block.tensor
                def _(pe):
                    def turn(b):
                        pe.wait_ge(scaled, b + 1)
                        need(pe, out, 2 * (b - 1))
                        for n in range(2):
                            for j in range(4):
                                k = 4 * n + j
                                x_ = nc.tensor.transpose(bank[4 + 2 * (b % 2) + n][:, j * P:(j + 1) * P], xs[:, b % 2, k * P:(k + 1) * P], ident[:])
                            x_.then_inc(turned, 1)

                    for b in range(R):
                        pe.wait_ge(staged, 2 * b + 2)
                        need(pe, ys if gated else added, 2 * (b - 1))
                        for n in range(2):
                            for k in range(KC):
                                if b == 0 and n == 0:
                                    pe.wait_ge(w_in[k], 16)
                                x_ = nc.tensor.matmul(bank[2 * (b % 2) + n][:], stage[:, b % 2, k], w[:, k, n * TB:(n + 1) * TB], start=(k == 0), stop=(k == KC - 1))
                            x_.then_inc(proj, 1)
                        if gated and b == 0:
                            pe.wait_ge(consts, 16 * 4)
                        if gated and b > 0:
                            turn(b - 1)
                    if gated:
                        turn(R - 1)

                if gated:
                    @block.scalar
                    def _(act):
                        for b in range(R):
                            h = b % 2
                            act.wait_ge(added, b + 1)
                            need(act, turned, 2 * (b - 1))
                            nc.scalar.activation(xs[:, h], y[:, h], ACT.Square, accum_out=st[:, b, 0:1]).then_inc(squared, 1)
                            act.wait_ge(squared, 2 * b + 1)
                            nc.scalar.activation(st[:, b, 1:2], st[:, b, 0:1], ACT.Sqrt, bias=epst[:, 0:1], scale=1.0 / D).then_inc(rooted, 1)
                            act.wait_ge(normed, b + 1)
                            nc.scalar.activation(xs[:, h], y[:, h], ACT.Square, accum_out=st[:, b, 3:4]).then_inc(squared, 1)
                            act.wait_ge(squared, 2 * b + 2)
                            nc.scalar.activation(st[:, b, 4:5], st[:, b, 3:4], ACT.Sqrt, bias=epst[:, 0:1], scale=1.0 / D).then_inc(rooted, 1)
                            act.wait_ge(recip, 2 * b + 2)
                            nc.scalar.activation(xs[:, h], y[:, h], ACT.Copy, scale=st[:, b, 5:6]).then_inc(scaled, 1)

                @block.vector
                def _(dve):
                    def put(b):
                        for n in range(2):
                            dve.wait_ge(turned, 2 * b + n + 1)
                            nc.vector.tensor_tensor(hT2[:, 4 * n:4 * n + 4, bass.ds(i * R * P + b * P, P)], bank[4 + 2 * (b % 2) + n][:, :].rearrange("p (k q) -> p k q", q=P),
                                                    nw[:, 4 * n:4 * n + 4].unsqueeze(2).broadcast_to([P, 4, P]), ALU.mult).then_inc(out, 1)

                    for b in range(R):
                        h = b % 2
                        need(dve, stored[h], 16 * (b // 2))
                        if gated:
                            need(dve, scaled, b - 1)
                        for n in range(2):
                            cols = slice(n * TB, (n + 1) * TB)
                            dve.wait_ge(proj, 2 * b + n + 1)
                            if gated:
                                if b == 0 and n == 0:
                                    dve.wait_ge(consts, 16 * 4)
                                nc.vector.tensor_tensor(y[:, h, cols], bank[2 * h + n][:], gate_b[:, cols], ALU.mult).then_inc(ys, 1)
                            else:
                                dve.wait_ge(x_in[h], 16 * (b // 2 + 1))
                                nc.vector.tensor_tensor(y[:, h, cols], bank[2 * h + n][:], x[:, h, cols], ALU.add).then_inc(added, 1)
                        if gated:
                            dve.wait_ge(rooted, 2 * b + 1)
                            nc.vector.reciprocal(st[:, b, 2:3], st[:, b, 1:2]).then_inc(recip, 1)
                            dve.wait_ge(recip, 2 * b + 1)
                            nc.vector.scalar_tensor_tensor(out=y[:, h], in0=y[:, h], scalar=st[:, b, 2:3], in1=fw_b[:], op0=ALU.mult, op1=ALU.mult).then_inc(normed, 1)
                            dve.wait_ge(rooted, 2 * b + 2)
                            nc.vector.reciprocal(st[:, b, 5:6], st[:, b, 4:5]).then_inc(recip, 1)
                            if b > 0:
                                put(b - 1)
                    if gated:
                        put(R - 1)
            clear(nc, sems, first)
        clear(nc, sems, sems[0])


def dilated_units(dil):
    half = P // 2
    blocks = T // dil // half
    units = []
    for res in range(dil):
        for b in range(blocks):
            k0, k1 = max(b - 1, 0), min(b + 2, blocks)
            at, wide = (res * blocks + k0) * half, (k1 - k0) * half
            if b % 2 == 0:
                off = (k0 - b + 2) * half
            else:
                off = 0
            c = (res * blocks + b) // 2
            if b % 2 == 0:
                chunks = ([(0, c - 1)] if b > 0 else []) + [(1, c)]
            else:
                chunks = [(0, c)] + ([(1, c + 1)] if b < blocks - 1 else [])
            units.append((res * blocks + b, [(at, wide, 0)], off, wide, chunks, (k0 - b + 1) * half, 0))
    return units


def dilated_attention(nc, t, hT, mix):
    half = P // 2
    U = T // half
    NU = N_CFG * U
    units = [dilated_units(dil) for dil in DILATIONS]
    wide = 3 * half
    with ExitStack() as ctx:
        sems = []
        sb, ps, sem = open_memory(nc, ctx, sems)
        consts = sem("d_consts")
        once = sem("d_once")
        first = bias_in = sem("d_bias_in")
        at = Attend(nc, ctx, sems, "da", wide, 2 * P, 4, NU)
        K_, Q_, V_, G_ = range(4)
        w = sb("w6", [P, 4, KC, P])
        kT = sb("kT6", [P, T])
        qbd = sb("qbd6", [P, U, P])
        vals = sb("vals6", [P, NT, P])
        o = sb("o6", [P, N_CFG, T])
        alpha = sb("alpha6", [P, N_CFG, TB])
        alphas = [alpha, kT[:, 0:N_CFG * TB].rearrange("p (c n) -> p c n", c=N_CFG)]
        sg = sb("sg6", [P, 2, TB])
        sq = sb("sq6", [P, 2, TB])
        rt = sb("rt6", [P, 2, TB])
        qn = sb("qn6", [P, 2, TB])
        bias = sb("bias6", [P, N_CFG, wide])
        ident = sb("ident6", [P, P])
        ones = sb("ones6", [P, P])
        qk_w = sb("qk_w6", [P, 2, N_CFG * PAIRS])
        epst = sb("eps6", [P, 1])
        lse = sb("lse6", [P, U])
        lse_sum = sb("lse_sum6", [P, U])
        lse_c = sb("lse_c6", [P, 8, U])
        bank = [ps(f"d{i}", [P, TB]) for i in range(8)]
        w_in = [sem(f"d_w{i}") for i in range(4)]
        w_next = [sem(f"d_wn{i}") for i in range(4)]
        proj = sem("d_proj")
        squared = sem("d_squared")
        ssq = sem("d_ssq")
        rooted = sem("d_rooted")
        recip = sem("d_recip")
        k_out = sem("d_k_out")
        q_out = sem("d_q_out")
        q_placed = sem("d_q_placed")
        v_out = sem("d_v_out")
        logged = sem("d_logged")
        lse_out = sem("d_lse_out")
        lse_stored = sem("d_lse_stored")
        lse_in = sem("d_lse_in")
        al_dve = sem("d_al_dve")
        al_act = sem("d_al_act")
        al_stored = sem("d_al_stored")
        al_in = [sem("d_al_in0"), sem("d_al_in1")]
        g_out = sem("d_g_out")
        weighed = sem("d_weighed")
        weighed_dve = sem("d_weighed_dve")
        summed = sem("d_summed")
        mixed = sem("d_mixed")
        w_v = t["w_in_2"].rearrange("(k p) n -> p k n", p=P)
        G0 = 2 * HALF + 3 * QKV

        def col(c, s):
            return G0 if s == G_ else 2 * HALF + {Q_: 0, K_: 1, V_: 2}[s] * QKV + c * HALF

        with nc.Block() as block:
            @block.sync
            def _(sp):
                sp.dma_start(ident[:], t["ident"]).then_inc(consts, 16)
                sp.dma_start(ones[:], t["block_ones"]).then_inc(consts, 16)
                for n, name in enumerate(("q_norm_w_2", "k_norm_w_2")):
                    sp.dma_start(qk_w[:, n], t[name].rearrange("(m s) d -> (s d) m", s=2), allow_slow_non_contiguous=True).then_inc(consts, 16)
                for s in (K_, Q_, V_):
                    sp.dma_start(w[:, s], w_v[:, :, col(0, s) + HALF - P:col(0, s) + HALF]).then_inc(consts, 16)
                sp.wait_ge(consts, 7 * 16)

            @block.gpsimd
            def _(pool):
                nc.gpsimd.memset(qbd[:], 0.0).then_inc(once, 1)
                nc.gpsimd.memset(at.p[:], 0.0).then_inc(once, 1)
                nc.gpsimd.memset(epst[:], EPS).then_inc(once, 1)

            @block.vector
            def _(dve):
                dve.wait_ge(consts, 7 * 16)
                nc.vector.tensor_scalar(qk_w[:, 0], qk_w[:, 0], -float(half) ** -0.5, None, ALU.mult).then_inc(once, 1)

        with nc.Fori(0, PAIRS) as back:
            g = (PAIRS - 1) - back
            with nc.Block() as block:
                def store_lse(sp, c):
                    sp.wait_ge(lse_out, c + 1)
                    dst = t["lse"][c].rearrange("h (b q r) -> h q r b", q=half, r=DILATIONS[c])
                    for h in range(2):
                        src = lse_sum[h * half:(h + 1) * half, :].rearrange("p (r b) -> p r b", r=DILATIONS[c])
                        sp.dma_start(dst[h], src, allow_slow_non_contiguous=True).then_inc(lse_stored, 16)

                def root(act, c, n):
                    m = 8 * c + n
                    act.wait_ge(ssq, m + 1)
                    need(act, k_out, min(4 * c + n - 1, 4 * c + 4))
                    need(act, q_out, 4 * c + max(n - 5, 0))
                    nc.scalar.activation(rt[:, n % 2], bank[4 + n % 2][:], ACT.Sqrt, bias=epst[:, 0:1], scale=1.0 / half).then_inc(rooted, 1)

                @block.sync
                def _(sp):
                    sp.dma_start(bias[:], t["alibi"][bass.ds(g, 1)].rearrange("g q c k -> (g q) c k")).then_inc(bias_in, 16)
                    for c in range(N_CFG):
                        for s in (K_, Q_, V_):
                            sp.wait_ge(proj, 12 * c + 4 * s + 4)
                            if c + 1 < N_CFG:
                                sp.dma_start(w[:, s], w_v[:, :, bass.ds(g * P + col(c + 1, s), P)]).then_inc(w_in[s], 16)
                            else:
                                sp.dma_start(w[:, s], w_v[:, :, bass.ds((PAIRS - 2 - back) * P + col(0, s), P)]).then_inc(w_next[s], 16)
                        if c == 0:
                            sp.dma_start(w[:, G_], w_v[:, :, bass.ds(g * P + col(0, G_), P)]).then_inc(w_in[G_], 16)
                        store_lse(sp, c)
                    sp.wait_ge(lse_stored, 32 * N_CFG)
                    for c in range(N_CFG):
                        sp.dma_start(lse_c[:, c], t["lse"][c].rearrange("h (q j) -> (h q) j", q=half)).then_inc(lse_in, 16)
                    sp.wait_ge(al_dve, 11)
                    for c in range(N_CFG):
                        sp.dma_start(t["alpha"][c].rearrange("h (q j) -> (h q) j", q=half), lse_c[:, 3 + c]).then_inc(al_stored, 16)
                    sp.wait_ge(al_stored, 16 * N_CFG)
                    for tb in range(NTB):
                        need(sp, weighed, tb - 1)
                        need(sp, weighed_dve, tb - 1)
                        for h in range(2):
                            src = t["alpha"][:, h, tb * TB:(tb + 1) * TB]
                            sp.dma_start(alphas[tb % 2][h * half:(h + 1) * half], src.partition_broadcast(half)).then_inc(al_in[tb % 2], 16)
                    for s in (K_, Q_, V_):
                        sp.wait_ge(w_next[s], 16)

                @block.gpsimd
                def _(pool):
                    for c, dil in enumerate(DILATIONS):
                        for tb in range(NTB):
                            pool.wait_ge(q_out, 4 * c + tb + 1)
                            for h in range(2):
                                rows = slice(h * half, (h + 1) * half)
                                src = qn[rows, tb % 2].rearrange("p (j r) -> p r j", r=dil)
                                dst = qbd[rows, :, h * half:(h + 1) * half]
                                if dil == 1:
                                    dst = dst[:, 8 * tb:8 * tb + 8]
                                    src = src.rearrange("p r (b q) -> p (r b) q", q=half)
                                elif dil == 4:
                                    dst = dst.rearrange("p (r b) q -> p r b q", r=dil)[:, :, 2 * tb:2 * tb + 2]
                                    src = src.rearrange("p r (b q) -> p r b q", q=half)
                                else:
                                    q0 = (tb % 2) * (TB // dil)
                                    dst = dst.rearrange("p (r b) q -> p r b q", r=dil)[:, :, tb // 2, q0:q0 + TB // dil]
                                nc.gpsimd.tensor_copy(dst, src).then_inc(q_placed, 1)
                        attend_pool(nc, pool, at, units[c], c * U)
                    for tb in range(NTB):
                        pool.wait_ge(al_in[tb % 2], 32 * (tb // 2 + 1))
                        part = o[:, 0:2, tb * TB:(tb + 1) * TB]
                        nc.gpsimd.tensor_tensor(part, part, alphas[tb % 2][:, 0:2], ALU.mult).then_inc(weighed, 1)

                @block.tensor
                def _(pe):
                    def sums(n):
                        pe.wait_ge(squared, n + 1)
                        need(pe, rooted, n - 1)
                        nc.tensor.matmul(bank[4 + n % 2][:], ones[:], sq[:, n % 2], start=True, stop=True).then_inc(ssq, 1)

                    for c, dil in enumerate(DILATIONS):
                        for n in range(12):
                            s, tb = divmod(n, 4)
                            if tb == 0 and c > 0:
                                pe.wait_ge(w_in[s], 16 * c)
                            if n < 4:
                                need(pe, at.biased, c * U)
                            elif n < 8:
                                pe.wait_ge(k_out, 4 * c + n - 3)
                            else:
                                pe.wait_ge(q_out, 4 * c + n - 7)
                            if s < V_:
                                for k in range(KC):
                                    x = nc.tensor.matmul(bank[n % 4][:], w[:, s, k], hT[:, k, tb * TB:(tb + 1) * TB], start=(k == 0), stop=(k == KC - 1))
                            else:
                                for j in range(4):
                                    res, j0 = divmod((4 * tb + j) * P, T // dil)
                                    for k in range(KC):
                                        toks = hT[:, k].rearrange("p (j r) -> p r j", r=dil)[:, res, j0:j0 + P]
                                        x = nc.tensor.matmul(bank[n % 4][:, j * P:(j + 1) * P], toks, w[:, s, k], start=(k == 0), stop=(k == KC - 1))
                            x.then_inc(proj, 1)
                            if 1 <= n < 9:
                                sums(8 * c + n - 1)
                        pe.wait_ge(q_placed, 8 * c + 8)
                        pe.wait_ge(v_out, 4 * c + 4)
                        attend_pe(nc, pe, at, units[c], c * U, bank, qbd, kT, vals, ident)
                    pe.wait_ge(w_in[G_], 16)
                    for tb in range(NTB):
                        if tb == 0:
                            pe.wait_ge(at.biased, NU)
                        for k in range(KC):
                            x = nc.tensor.matmul(bank[tb][:], w[:, G_, k], hT[:, k, tb * TB:(tb + 1) * TB], start=(k == 0), stop=(k == KC - 1))
                        x.then_inc(proj, 1)

                @block.scalar
                def _(act):
                    for c in range(N_CFG):
                        for n in range(8):
                            m = 8 * c + n
                            act.wait_ge(proj, 12 * c + n + 1)
                            need(act, ssq, m - 1)
                            nc.scalar.activation(sq[:, n % 2], bank[n % 4][:], ACT.Square).then_inc(squared, 1)
                            if n >= 1:
                                root(act, c, n - 1)
                        root(act, c, 7)
                        for n in range(4):
                            act.wait_ge(proj, 12 * c + 9 + n)
                            nc.scalar.copy(vals[:, 4 * n:4 * n + 4], bank[n][:, :].rearrange("p (c l) -> p c l", l=P)).then_inc(v_out, 1)
                        attend_act(nc, act, at, units[c], c * U, bank)
                        act.wait_ge(at.exped, (c + 1) * U)
                        need(act, lse_out, c)
                        nc.scalar.activation(lse[:], at.total[:, c * U:(c + 1) * U], ACT.Ln).then_inc(logged, 1)
                    for c in range(N_CFG):
                        act.wait_ge(al_dve, 2 + 3)
                        nc.scalar.activation(lse_c[:, 3 + c], lse_c[:, 3 + c], ACT.Exp).then_inc(al_act, 1)
                    for tb in range(NTB):
                        act.wait_ge(proj, 36 + tb + 1)
                        need(act, mixed, tb - 1)
                        nc.scalar.activation(sg[:, tb % 2], bank[tb][:], ACT.Silu).then_inc(g_out, 1)

                @block.vector
                def _(dve):
                    for c, dil in enumerate(DILATIONS):
                        for n in range(8):
                            m = 8 * c + n
                            tb = n % 4
                            dve.wait_ge(rooted, m + 1)
                            nc.vector.reciprocal(rt[:, n % 2], rt[:, n % 2]).then_inc(recip, 1)
                            dve.wait_ge(recip, m + 1)
                            wt = qk_w[:, 1 if n < 4 else 0, bass.ds(c * PAIRS + g, 1)]
                            if n < 4:
                                if n == 0 and c > 0:
                                    dve.wait_ge(at.qk, c * U)
                                n_j = TB // dil
                                dst = kT[:, :].rearrange("p (r j) -> p r j", r=dil)[:, :, tb * n_j:(tb + 1) * n_j]
                                view = lambda x: x.rearrange("p (j r) -> p r j", r=dil)
                                nc.vector.scalar_tensor_tensor(out=dst, in0=view(bank[n % 4][:, :]), scalar=wt, in1=view(rt[:, n % 2]), op0=ALU.mult, op1=ALU.mult).then_inc(k_out, 1)
                            else:
                                need(dve, q_placed, 8 * c + 2 * (tb - 1))
                                nc.vector.scalar_tensor_tensor(out=qn[:, n % 2], in0=bank[n % 4][:], scalar=wt, in1=rt[:, n % 2], op0=ALU.mult, op1=ALU.mult).then_inc(q_out, 1)
                        if c == 0:
                            dve.wait_ge(bias_in, 16)

                        def bias_of(unit):
                            return bias[:, c, unit[5]:unit[5] + unit[3]]

                        def write_out(b):
                            dve.wait_ge(at.pv, 4 * b + 4)
                            for h in range(2):
                                rows = slice(h * half, (h + 1) * half)
                                src = bank[6 + b % 2][rows, :].rearrange("p (u q) -> p u q", q=P)[:, :, h * half:(h + 1) * half]
                                j0 = 4 * (b - c * U // 4) * half
                                res, j = divmod(j0, T // dil)
                                dst = o[rows, c].rearrange("p (j r) -> p r j", r=dil)
                                if dil <= 4:
                                    dst = dst[:, res, j:j + 4 * half].rearrange("p (u q) -> p u q", q=half)
                                else:
                                    dst = dst[:, res:res + 2]
                                    dst = dst.rearrange("p r (b q) -> p r b q", q=half)
                                    src = src.rearrange("p (r b) q -> p r b q", r=2)
                                nc.vector.tensor_copy(dst, src).then_inc(at.out, 1)

                        attend_dve(nc, dve, at, units[c], c * U, bank, bias_of, write_out)
                        dve.wait_ge(logged, c + 1)
                        need(dve, lse_stored, 32 * c)
                        nc.vector.tensor_tensor(lse_sum[:], lse[:], at.negmax[:, c * U:(c + 1) * U], ALU.subtract).then_inc(lse_out, 1)
                    dve.wait_ge(lse_in, 16 * N_CFG)
                    nc.vector.tensor_tensor(lse_c[:, 6], lse_c[:, 0], lse_c[:, 1], ALU.max).then_inc(al_dve, 1)
                    dve.wait_ge(al_dve, 1)
                    nc.vector.tensor_tensor(lse_c[:, 7], lse_c[:, 6], lse_c[:, 2], ALU.max).then_inc(al_dve, 1)
                    dve.wait_ge(al_dve, 2)
                    for c in range(N_CFG):
                        nc.vector.tensor_tensor(lse_c[:, 3 + c], lse_c[:, c], lse_c[:, 7], ALU.subtract).then_inc(al_dve, 1)
                    dve.wait_ge(al_act, 3)
                    nc.vector.tensor_tensor(lse_c[:, 0], lse_c[:, 3], lse_c[:, 4], ALU.add).then_inc(al_dve, 1)
                    dve.wait_ge(al_dve, 6)
                    nc.vector.tensor_tensor(lse_c[:, 1], lse_c[:, 0], lse_c[:, 5], ALU.add).then_inc(al_dve, 1)
                    dve.wait_ge(al_dve, 7)
                    nc.vector.reciprocal(lse_c[:, 2], lse_c[:, 1]).then_inc(al_dve, 1)
                    dve.wait_ge(al_dve, 8)
                    for c in range(N_CFG):
                        nc.vector.tensor_tensor(lse_c[:, 3 + c], lse_c[:, 3 + c], lse_c[:, 2], ALU.mult).then_inc(al_dve, 1)
                    for tb in range(NTB):
                        cols = slice(tb * TB, (tb + 1) * TB)
                        dve.wait_ge(al_in[tb % 2], 32 * (tb // 2 + 1))
                        nc.vector.tensor_tensor(o[:, 2, cols], o[:, 2, cols], alphas[tb % 2][:, 2], ALU.mult).then_inc(weighed_dve, 1)
                        dve.wait_ge(weighed, tb + 1)
                        nc.vector.tensor_tensor(o[:, 0, cols], o[:, 0, cols], o[:, 1, cols], ALU.add).then_inc(summed, 1)
                        dve.wait_ge(summed, 2 * tb + 1)
                        dve.wait_ge(weighed_dve, tb + 1)
                        nc.vector.tensor_tensor(o[:, 0, cols], o[:, 0, cols], o[:, 2, cols], ALU.add).then_inc(summed, 1)
                        dve.wait_ge(g_out, tb + 1)
                        dve.wait_ge(summed, 2 * tb + 2)
                        nc.vector.tensor_tensor(mix[:, bass.ds(g, 1), cols][:, 0], o[:, 0, cols], sg[:, tb % 2], ALU.mult).then_inc(mixed, 1)
            clear(nc, sems, first)
        clear(nc, sems, sems[0])


def fourier(nc, t, hT, mix):
    M = T // 2
    MC = M // P
    with ExitStack() as ctx:
        sems = []
        sb, ps, sem = open_memory(nc, ctx, sems)
        consts = sem("f_consts")
        once = sem("f_once")
        U_, G_ = range(2)
        w = sb("w5", [P, 2, KC, P])
        u = sb("u5", [P, T])
        ue = sb("ue5", [P, 2, M])
        trig = sb("trig5", [P, 4, 2, M])
        chan = sb("chan5", [P, 2, P])
        wd = sb("wd5", [P, P])
        ab = sb("ab5", [P, 2, P])
        co = sb("co5", [P, 2, MC, P])
        mid = sb("mid5", [1, P])
        alt_row = sb("alt_row", [1, M])
        alt_col = sb("alt_col", [P, 1])
        one = sb("one5", [1, 1])
        qs = sb("qs5", [P, M])
        f = u
        bank = [ps(f"f{i}", [P, TB]) for i in range(8)]
        w_in = [sem(f"f_w{i}") for i in range(2)]
        first = w_in[0]
        wd_in = sem("f_wd_in")
        trig_in = [sem(f"f_trig{i}") for i in range(4)]
        proj = sem("f_proj")
        out_act = sem("f_out_act")
        ab_done = sem("f_ab_done")
        ab_out = sem("f_ab_out")
        folded = sem("f_folded")
        zeroed = sem("f_zeroed")
        coef = sem("f_coef")
        co_out = sem("f_co_out")
        trig_used = sem("f_trig_used")
        done = sem("f_done")
        qs_out = sem("f_qs_out")
        joined = sem("f_joined")
        mixed = sem("f_mixed")
        w_v = t["w_in_2"].rearrange("(k p) n -> p k n", p=P)
        half = P // 2
        with nc.Block() as block:
            @block.sync
            def _(sp):
                sp.dma_start(chan[:], t["chan_trig"]).then_inc(consts, 16)
                sp.dma_start(alt_row[:], t["alternate"]).then_inc(consts, 16)
                sp.dma_start(alt_col[:], t["alternate"][0, 0:P].unsqueeze(1)).then_inc(consts, 16)
                for s in range(2):
                    sp.dma_start(w[:, s], w_v[:, :, s * HALF:s * HALF + P]).then_inc(consts, 16)
                sp.wait_ge(consts, 5 * 16)

            @block.gpsimd
            def _(pool):
                nc.gpsimd.memset(wd[:], 0.0).then_inc(once, 1)
                nc.gpsimd.memset(one[:], 1.0).then_inc(once, 1)
                nc.gpsimd.memset(ue[:], 0.0).then_inc(once, 1)

        with nc.Fori(0, PAIRS) as g:
            with nc.Block() as block:
                @block.sync
                def _(sp):
                    for h in range(2):
                        rows = slice(h * half, (h + 1) * half)
                        sp.dma_start(wd[rows, h * half:(h + 1) * half], t["w_fourier_2"][bass.ds(2 * g + h, 1)].rearrange("a c d -> (a c) d")).then_inc(wd_in, 16)
                    for k in range(4):
                        sp.dma_start(trig[:, k], t["trig"][k]).then_inc(trig_in[k], 16)
                    for s in range(2):
                        sp.wait_ge(proj, 4 * s + 4)
                        sp.dma_start(w[:, s], w_v[:, :, bass.ds((g + 1) * P + s * HALF, P)]).then_inc(w_in[s], 16)
                    for k in range(4, MC):
                        sp.wait_ge(trig_used, k - 3)
                        sp.dma_start(trig[:, k % 4], t["trig"][k]).then_inc(trig_in[k % 4], 16)
                    for s in range(2):
                        sp.wait_ge(w_in[s], 16)

                @block.tensor
                def _(pe):
                    for n in range(8):
                        s, tb = divmod(n, 4)
                        need(pe, out_act, n - 3)
                        for k in range(KC):
                            x = nc.tensor.matmul(bank[n % 4][:], w[:, s, k], hT[:, k, tb * TB:(tb + 1) * TB], start=(k == 0), stop=(k == KC - 1))
                        x.then_inc(proj, 1)
                        if n == 3:
                            pe.wait_ge(wd_in, 32)
                            for i in range(2):
                                x = nc.tensor.matmul(bank[4][:, i * P:(i + 1) * P], chan[:, i], wd[:], start=True, stop=True)
                            x.then_inc(ab_done, 1)
                    pe.wait_ge(ab_out, 1)
                    for i in range(2):
                        pe.wait_ge(folded, 1 + i)
                        for m in range(MC):
                            x = nc.tensor.matmul(bank[4 + 2 * i + m // 4][:, (m % 4) * P:(m % 4 + 1) * P], ue[:, i, m * P:(m + 1) * P], ab[:, i], start=True, stop=True)
                        x.then_inc(coef, 1)
                    pe.wait_ge(out_act, 8)
                    nc.tensor.matmul(bank[0][0:1, 0:P], u[:, M:M + 1], ab[:, 0], start=True, stop=True).then_inc(coef, 1)
                    pe.wait_ge(co_out, 5)
                    for n in range(2):
                        nc.tensor.matmul(bank[n][:], mid[0:1, :], alt_row[0:1, n * TB:(n + 1) * TB], start=True, stop=False)
                    nc.tensor.matmul(bank[4][:, 0:1], mid[0:1, :], one[0:1, :], start=True, stop=False)
                    for k in range(MC):
                        pe.wait_ge(trig_in[k % 4], 16 * (k // 4 + 1))
                        for i in range(2):
                            for n in range(2):
                                x = nc.tensor.matmul(bank[2 * i + n][:], co[:, i, k], trig[:, k % 4, i, n * TB:(n + 1) * TB], start=(i == 1 and k == 0), stop=(k == MC - 1))
                        x.then_inc(trig_used, 1)
                        x = nc.tensor.matmul(bank[4][:, 0:1], co[:, 0, k], alt_col[:], start=False, stop=(k == MC - 1))
                    x.then_inc(done, 1)

                @block.scalar
                def _(act):
                    for n in range(8):
                        s, tb = divmod(n, 4)
                        b = slice(tb * TB, (tb + 1) * TB)
                        act.wait_ge(proj, n + 1)
                        if s == U_:
                            nc.scalar.copy(u[:, b], bank[n % 4][:]).then_inc(out_act, 1)
                        else:
                            nc.scalar.activation(mix[:, bass.ds(g, 1), b][:, 0], bank[n % 4][:], ACT.Silu).then_inc(out_act, 1)
                        if n == 3:
                            act.wait_ge(out_act, 4)
                            nc.scalar.copy(ue[:, 0, 0:1], u[:, 0:1]).then_inc(zeroed, 1)
                            act.wait_ge(ab_done, 1)
                            nc.scalar.copy(ab[:], bank[4][:, 0:2 * P].rearrange("p (i c) -> p i c", i=2)).then_inc(ab_out, 1)
                    for i in range(2):
                        act.wait_ge(coef, i + 1)
                        for n in range(2):
                            nc.scalar.copy(co[:, i, 4 * n:4 * n + 4], bank[4 + 2 * i + n][:, :].rearrange("p (m c) -> p m c", c=P)).then_inc(co_out, 1)
                    act.wait_ge(coef, 3)
                    nc.scalar.copy(mid[:], bank[0][0:1, 0:P]).then_inc(co_out, 1)
                    act.wait_ge(done, 1)
                    for n in range(2):
                        nc.scalar.copy(qs[:, n * TB:(n + 1) * TB], bank[2 + n][:]).then_inc(qs_out, 1)
                    nc.scalar.copy(f[:, M:M + 1], bank[4][:, 0:1]).then_inc(qs_out, 1)

                @block.vector
                def _(dve):
                    dve.wait_ge(zeroed, 1)
                    for i, op in enumerate((ALU.add, ALU.subtract)):
                        nc.vector.tensor_tensor(ue[:, i, 1:M], u[:, 1:M], u[:, T - 1:M:-1], op).then_inc(folded, 1)
                    for n in range(2):
                        dve.wait_ge(qs_out, 3)
                        cols = slice(n * TB, (n + 1) * TB)
                        nc.vector.tensor_tensor(f[:, cols], bank[n][:], qs[:, cols], ALU.subtract).then_inc(joined, 1)
                        s0, s1 = max(n * TB, 1), (n + 1) * TB
                        nc.vector.tensor_tensor(f[:, T - s0:T - s1:-1], bank[n][:, s0 - n * TB:], qs[:, s0:s1], ALU.add).then_inc(joined, 1)
                    dve.wait_ge(joined, 4)
                    dve.wait_ge(out_act, 8)
                    ml = mix[:, bass.ds(g, 1)][:, 0]
                    nc.vector.tensor_tensor(ml, f[:], ml, ALU.mult).then_inc(mixed, 1)
            clear(nc, sems, first)
        clear(nc, sems, sems[0])


def shape_constants():
    idx = np.arange(P)
    ident = np.eye(P, dtype=np.float32)
    pick = np.zeros((P, 2, P), np.float32)
    pick[P - 1, 0] = 1.0
    pick[0, 1] = 1.0
    fresh = np.ones((1, T), np.float32)
    fresh[0, ::P] = 0.0
    causal = np.zeros((P, 2, P), np.float32)
    causal[:, 0][idx[:, None] > idx[None, :]] = -BIG
    causal[:, 1][idx[:, None] < idx[None, :]] = -BIG
    key, query = np.arange(GRID_W)[None, :], np.arange(GRID_W)[:, None]
    first = np.clip(query - NA_KW // 2, 0, GRID_W - NA_KW)
    seen = (key >= first) & (key < first + NA_KW)
    na_mask = np.tile(np.where(seen, 0.0, BIG).astype(np.float32), (2, 1))
    half = P // 2
    block_ones = np.kron(np.eye(2), np.ones((half, half))).astype(np.float32)
    slot = np.arange(2 * PAIRS).reshape(PAIRS, 2, 1, 1, 1)
    slope = 2.0 ** (-8.0 * (slot + 1) / (2 * PAIRS))
    dil = np.array(DILATIONS).reshape(1, 1, 1, N_CFG, 1)
    rel = np.abs(np.arange(3 * half)[None, :] - half - np.arange(half)[:, None]).reshape(1, 1, half, 1, 3 * half)
    alibi = np.where(rel <= half, slope * dil * rel, BIG).astype(np.float32).reshape(PAIRS, P, N_CFG, 3 * half)
    M = T // 2
    turn = (np.arange(M)[:, None] * np.arange(M)[None, :]) % T
    angle = turn * (2 * np.pi / T)
    trig = np.stack([np.cos(angle), np.sin(angle)], axis=1).astype(np.float32).reshape(M // P, P, 2, M)
    small = (np.arange(half)[:, None] * np.arange(half)[None, :]) % half * (2 * np.pi / half)
    scale = 1.0 / np.sqrt(T * half)
    chan = np.stack([np.kron(np.eye(2), np.cos(small)), np.kron(np.eye(2), np.sin(small))], axis=1) * scale
    alternate = np.where(np.arange(M) % 2, -1.0, 1.0).astype(np.float32)[None, :]
    return {"block_ones": block_ones, "alibi": alibi, "trig": trig, "chan_trig": chan.astype(np.float32),
            "alternate": alternate, "na_mask": na_mask, "ident": ident, "pick": pick, "fresh": fresh, "causal": causal}


def build(nc, t):
    with ExitStack() as ctx:
        sb, _, _ = open_memory(nc, ctx)
        hT = sb("hT", [P, KC, T])
        modulate_and_norm(nc, t, hT)
        mix_ml = sb("mix_ml", [P, ML_HEADS, T])
        with ExitStack() as inner:
            sb_in, _, _ = open_memory(nc, inner)
            gates = sb_in("gates", [P, NT, 2, 4, ML_HEADS])
            decay = sb_in("decay", [P, 2, NT, ML_HEADS])
            gate_rows(nc, t, hT, gates, decay)
            mlstm(nc, t, hT, mix_ml, gates, decay)
        with ExitStack() as inner:
            sb_in, _, _ = open_memory(nc, inner)
            mix_na = sb_in("mix_na", [P, PAIRS, T])
            grid_attention(nc, t, hT, mix_na)
            project_out(nc, t, (mix_na, mix_ml), True, hT)
        dilated_attention(nc, t, hT, mix_ml)
        mix_f = sb("mix_f", [P, PAIRS, T])
        fourier(nc, t, hT, mix_f)
        project_out(nc, t, (mix_f, mix_ml), False, None)


INPUTS = ["x", "c", "w_ada", "b_ada", "norm_w", "w_in", "b_in", "conv_w", "conv_b", "rpb", "ml_norm_w", "w_out", "final_norm_w",
          "norm_w_2", "w_in_2", "q_norm_w_2", "k_norm_w_2", "w_fourier_2", "w_out_2"]
SCRATCH = {
    "gate_row": (1, D),
    "r_rows": (2, ML_HEADS, T),
    "rpb_pad": (1, 2 * RPB_PAD + 2 * PAIRS * NDY * NDX),
    "rpb_rows": (PAIRS, 2, GRID_W, NDY, GRID_W),
    "x1": (T, D),
    "lse": (N_CFG, 2, T),
    "alpha": (N_CFG, 2, T),
}


def kernel(**inputs):
    import concourse.bacc as bacc
    from concourse.bass_utils import run_bass_kernel_spmd

    nc = bacc.Bacc("TRN2", target_bir_lowering=False, num_devices=1)
    arrays = {name: np.ascontiguousarray(inputs[name]) for name in INPUTS} | shape_constants()
    t = {name: nc.dram_tensor("in_" + name, a.shape, F32, kind="ExternalInput").ap() for name, a in arrays.items()}
    t |= {name: nc.dram_tensor(name, shape, F32, kind="Internal").ap() for name, shape in SCRATCH.items()}
    t["out"] = nc.dram_tensor("out_0", (1, T, D), F32, kind="ExternalOutput").ap()
    build(nc, t)
    result = run_bass_kernel_spmd(nc, [{"in_" + name: a for name, a in arrays.items()}], core_ids=[0])
    return result.results[0]["out_0"]
```
